# Optimizing a Trainium2 kernel written in Bass

```python
import math
import jax, jax.numpy as jnp
from jax import lax
import numpy as np

D_MODEL = 1024
BATCH = 1
SEQ = 512
DEPTH = 1

CHUNK = 64
HEAD_DIM = 64
N_HEADS_FOX = 8
N_HEADS_CHUNK = 8
WIDTH_FOX = N_HEADS_FOX * HEAD_DIM
WIDTH_CHUNK = N_HEADS_CHUNK * HEAD_DIM
LEFT_CHUNKS = 8
BAND_CHUNKS = LEFT_CHUNKS + 1
REL_CLIP = 128
Q_BLOCK = 128
D_FF = 2816
CONV_WIDTH = 3
LN_EPS = 1e-5
N_MOD = 6
PROJ_SIZES = (WIDTH_FOX, WIDTH_FOX, WIDTH_FOX, N_HEADS_FOX,
              WIDTH_CHUNK, WIDTH_CHUNK, WIDTH_CHUNK, D_MODEL, D_MODEL)
PROJ_COLS = sum(PROJ_SIZES)


def _layer_norm(x, gain=None, bias=None):
    xf = x.astype(jnp.float32)
    mu = jnp.mean(xf, axis=-1, keepdims=True)
    var = jnp.mean(jnp.square(xf - mu), axis=-1, keepdims=True)
    y = (xf - mu) * lax.rsqrt(var + LN_EPS)
    if gain is not None:
        y = y * gain.astype(jnp.float32) + bias.astype(jnp.float32)
    return y.astype(x.dtype)

def _forgetting_attention(q, k, v, f_logit):
    b, s, h, dh = q.shape
    n_blk = s // Q_BLOCK
    log_f = jax.nn.log_sigmoid(f_logit.astype(jnp.float32))
    cum = jnp.cumsum(log_f, axis=1).transpose(0, 2, 1)
    scale = 1.0 / math.sqrt(dh)
    k_pos = jnp.arange(s)
    q_blocks = q.reshape(b, n_blk, Q_BLOCK, h, dh).transpose(1, 0, 2, 3, 4)
    cum_blocks = cum.reshape(b, h, n_blk, Q_BLOCK).transpose(2, 0, 1, 3)
    neg = jnp.finfo(jnp.float32).min

    def block(args):
        qb, cq, i = args
        q_pos = i * Q_BLOCK + jnp.arange(Q_BLOCK)
        logits = jnp.einsum('bqhd,bkhd->bhqk', qb, k).astype(jnp.float32) * scale
        logits = logits + cq[:, :, :, None] - cum[:, :, None, :]
        mask = k_pos[None, :] <= q_pos[:, None]
        logits = jnp.where(mask[None, None], logits, neg)
        p = jax.nn.softmax(logits, axis=-1).astype(v.dtype)
        return jnp.einsum('bhqk,bkhd->bqhd', p, v)

    out = lax.map(block, (q_blocks, cum_blocks, jnp.arange(n_blk)))
    return out.transpose(1, 0, 2, 3, 4).reshape(b, s, h * dh)

def _chunk_band_attention(q, k, v, rel_table):
    b, s, h, dh = q.shape
    n_c = s // CHUNK
    band = BAND_CHUNKS * CHUNK
    qc = q.reshape(b, n_c, CHUNK, h, dh)
    pad = ((0, 0), (LEFT_CHUNKS, 0), (0, 0), (0, 0), (0, 0))
    kp = jnp.pad(k.reshape(b, n_c, CHUNK, h, dh), pad)
    vp = jnp.pad(v.reshape(b, n_c, CHUNK, h, dh), pad)
    band_idx = jnp.arange(n_c)[:, None] + jnp.arange(BAND_CHUNKS)[None, :]
    kb = kp[:, band_idx].reshape(b, n_c, band, h, dh)
    vb = vp[:, band_idx].reshape(b, n_c, band, h, dh)
    valid = jnp.repeat(band_idx >= LEFT_CHUNKS, CHUNK, axis=1)
    q_off = LEFT_CHUNKS * CHUNK + np.arange(CHUNK)
    rel = np.clip(q_off[:, None] - np.arange(band)[None, :], -REL_CLIP, REL_CLIP) + REL_CLIP
    bias = rel_table[:, rel].astype(jnp.float32)
    scale = 1.0 / math.sqrt(dh)
    logits = jnp.einsum('bcqhd,bckhd->bchqk', qc, kb).astype(jnp.float32) * scale
    logits = logits + bias[None, None]
    logits = jnp.where(valid[None, :, None, None, :], logits, jnp.finfo(jnp.float32).min)
    p = jax.nn.softmax(logits, axis=-1).astype(v.dtype)
    out = jnp.einsum('bchqk,bckhd->bcqhd', p, vb)
    return out.reshape(b, s, h * dh)

def _causal_depthwise_conv(u, w, bias):
    s = u.shape[1]
    up = jnp.pad(u, ((0, 0), (CONV_WIDTH - 1, 0), (0, 0)))
    y = bias
    for j in range(CONV_WIDTH):
        y = y + w[j] * up[:, j:j + s]
    return y

def first_inputs(seed: int = 0) -> dict:
    key = jax.random.key(seed)
    ks = jax.random.split(key, 20)
    beta = (8.0 * DEPTH) ** -0.25
    f32 = jnp.float32
    nrm = lambda k, shape: jax.random.normal(k, shape, f32)
    col_scale = np.concatenate([
        np.ones(2 * WIDTH_FOX), beta * np.ones(WIDTH_FOX), 0.5 * np.ones(N_HEADS_FOX),
        np.ones(2 * WIDTH_CHUNK), beta * np.ones(WIDTH_CHUNK), np.ones(2 * D_MODEL)]).astype(np.float32)
    w_in = nrm(ks[2], (DEPTH, D_MODEL, PROJ_COLS)) * (D_MODEL ** -0.5) * jnp.asarray(col_scale)
    b_f = jnp.linspace(1.0, 5.0, N_HEADS_FOX, dtype=f32)[None, :] + 0.1 * nrm(ks[3], (DEPTH, N_HEADS_FOX))
    rel_bias = 0.5 * nrm(ks[4], (DEPTH, N_HEADS_CHUNK, 2 * REL_CLIP + 1))
    w_br_fox = nrm(ks[5], (DEPTH, WIDTH_FOX, D_MODEL)) * WIDTH_FOX ** -0.5
    w_br_chunk = nrm(ks[6], (DEPTH, WIDTH_CHUNK, D_MODEL)) * WIDTH_CHUNK ** -0.5
    w_out = nrm(ks[7], (DEPTH, D_MODEL, D_MODEL)) * (D_MODEL ** -0.5) * beta
    w_up = nrm(ks[8], (DEPTH, D_MODEL, 2 * D_FF)) * D_MODEL ** -0.5
    conv_w = 0.3 * nrm(ks[9], (DEPTH, CONV_WIDTH, 2 * D_FF)) + jnp.array([0.0, 0.0, 1.0], f32)[None, :, None]
    conv_b = 0.01 * nrm(ks[10], (DEPTH, 2 * D_FF))
    w_down = nrm(ks[11], (DEPTH, D_FF, D_MODEL)) * (D_FF ** -0.5) * beta
    w_ada = 0.2 * nrm(ks[12], (DEPTH, D_MODEL, N_MOD * D_MODEL)) * D_MODEL ** -0.5
    b_ada = 0.01 * nrm(ks[13], (DEPTH, N_MOD * D_MODEL))
    ln1_g = 1.0 + 0.05 * nrm(ks[14], (DEPTH, D_MODEL))
    ln1_b = 0.01 * nrm(ks[15], (DEPTH, D_MODEL))
    ln2_g = 1.0 + 0.05 * nrm(ks[16], (DEPTH, D_MODEL))
    ln2_b = 0.01 * nrm(ks[17], (DEPTH, D_MODEL))
    x = nrm(ks[0], (BATCH, SEQ, D_MODEL))
    c = nrm(ks[1], (BATCH, D_MODEL))
    return {"x": x, "c": c, "w_in": w_in, "b_f": b_f, "rel_bias": rel_bias,
            "w_br_fox": w_br_fox, "w_br_chunk": w_br_chunk, "w_out": w_out,
            "w_up": w_up, "conv_w": conv_w, "conv_b": conv_b, "w_down": w_down,
            "w_ada": w_ada, "b_ada": b_ada, "ln1_g": ln1_g, "ln1_b": ln1_b,
            "ln2_g": ln2_g, "ln2_b": ln2_b}

def first_block(x, c, w_in, b_f, rel_bias, w_br_fox, w_br_chunk, w_out, w_up, conv_w,
              conv_b, w_down, w_ada, b_ada, ln1_g, ln1_b, ln2_g, ln2_b):
    alpha = (2.0 * DEPTH) ** 0.25
    b, s, _ = x.shape
    split_points = list(np.cumsum(PROJ_SIZES)[:-1])
    cond = jax.nn.silu(c)
    for l in range(DEPTH):
        mod = cond @ w_ada[l] + b_ada[l]
        sh1, sc1, g1, sh2, sc2, g2 = jnp.split(mod[:, None, :], N_MOD, axis=-1)

        h = _layer_norm(x) * (1.0 + sc1) + sh1
        proj = h @ w_in[l]
        q_a, k_a, v_a, f_a, q_c, k_c, v_c, gate_a, gate_c = jnp.split(proj, split_points, axis=-1)
        heads_a = lambda t: t.reshape(b, s, N_HEADS_FOX, HEAD_DIM)
        heads_c = lambda t: t.reshape(b, s, N_HEADS_CHUNK, HEAD_DIM)
        o_a = _forgetting_attention(heads_a(q_a), heads_a(k_a), heads_a(v_a), f_a + b_f[l])
        o_c = _chunk_band_attention(heads_c(q_c), heads_c(k_c), heads_c(v_c), rel_bias[l])
        merged = (jax.nn.sigmoid(gate_a) * (o_a @ w_br_fox[l])
                  + jax.nn.sigmoid(gate_c) * (o_c @ w_br_chunk[l]))
        mix = merged @ w_out[l]
        x = _layer_norm(alpha * x + (1.0 + g1) * mix, ln1_g[l], ln1_b[l])

        h = _layer_norm(x) * (1.0 + sc2) + sh2
        u = _causal_depthwise_conv(h @ w_up[l], conv_w[l], conv_b[l])
        a, val = jnp.split(u, 2, axis=-1)
        y = (jax.nn.silu(a) * val) @ w_down[l]
        x = _layer_norm(alpha * x + (1.0 + g2) * y, ln2_g[l], ln2_b[l])
    return x


N_META = 16
EPS = 1e-6
ATT_HEADS = 8
ATT_KV_HEADS = 2
ATT_HEAD_DIM = 64
WINDOW = 128
WINDOW_CHUNKS = WINDOW // CHUNK
GLA_HEADS = 4
GLA_DK = 64
GLA_DV = 128
GLA_GATE_RANK = 16
GLA_GATE_TEMP = 16.0

ATT_Q = ATT_HEADS * ATT_HEAD_DIM
ATT_KV = ATT_KV_HEADS * ATT_HEAD_DIM
GLA_QK = GLA_HEADS * GLA_DK
GLA_V = GLA_HEADS * GLA_DV
SPLITS = (ATT_Q, ATT_KV, ATT_KV, GLA_QK, GLA_QK, GLA_V, GLA_V, GLA_GATE_RANK, D_MODEL, D_MODEL)
D_IN = ATT_Q + 2 * ATT_KV + 2 * GLA_QK + 2 * GLA_V + GLA_GATE_RANK + 2 * D_MODEL


def rmsnorm(x, g):
    xf = x.astype(jnp.float32)
    y = xf * lax.rsqrt(jnp.mean(xf * xf, axis=-1, keepdims=True) + EPS)
    return (y * g.astype(jnp.float32)).astype(x.dtype)

def swiglu(x, w_gate, w_up, w_down):
    return (jax.nn.silu(x @ w_gate) * (x @ w_up)) @ w_down

def window_sink_attention(q, k, v, sinks):
    B, L = q.shape[0], q.shape[1]
    n_frames = L - N_META
    nc = n_frames // CHUNK
    G = ATT_HEADS // ATT_KV_HEADS
    NB = (WINDOW_CHUNKS + 1) * CHUNK
    pad = WINDOW_CHUNKS * CHUNK
    scale = ATT_HEAD_DIM ** -0.5
    slopes = jnp.exp2(-8.0 * jnp.arange(1, ATT_HEADS + 1, dtype=jnp.float32) / ATT_HEADS).reshape(ATT_KV_HEADS, G)
    sink = sinks.astype(jnp.float32).reshape(ATT_KV_HEADS, G)

    qm = q[:, :N_META].reshape(B, N_META, ATT_KV_HEADS, G, ATT_HEAD_DIM)
    qf = q[:, N_META:].reshape(B, nc, CHUNK, ATT_KV_HEADS, G, ATT_HEAD_DIM)
    km, kf = k[:, :N_META], k[:, N_META:]
    vm, vf = v[:, :N_META], v[:, N_META:]

    def band(t):
        tp = jnp.pad(t, ((0, 0), (pad, 0), (0, 0), (0, 0)))
        tp = tp.reshape(B, nc + WINDOW_CHUNKS, CHUNK, ATT_KV_HEADS, ATT_HEAD_DIM)
        return jnp.concatenate([tp[:, j:j + nc] for j in range(WINDOW_CHUNKS + 1)], axis=2)

    kb, vb = band(kf), band(vf)
    qi = jnp.arange(nc)[:, None] * CHUNK + jnp.arange(CHUNK)[None, :]
    ki = jnp.arange(nc)[:, None] * CHUNK - pad + jnp.arange(NB)[None, :]
    dist = jnp.abs(qi[:, :, None] - ki[:, None, :]).astype(jnp.float32)
    valid = (ki >= 0)[:, None, :]

    s_band = jnp.einsum('bcqkgd,bcskd->bkgcqs', qf, kb).astype(jnp.float32) * scale
    s_band = s_band - slopes[None, :, :, None, None, None] * dist[None, None, None]
    s_band = jnp.where(valid, s_band, -jnp.inf)
    s_meta = jnp.einsum('bcqkgd,bmkd->bkgcqm', qf, km).astype(jnp.float32) * scale
    s_sink = jnp.broadcast_to(sink[None, :, :, None, None, None], (B, ATT_KV_HEADS, G, nc, CHUNK, 1))
    p = jax.nn.softmax(jnp.concatenate([s_meta, s_band, s_sink], axis=-1), axis=-1).astype(v.dtype)
    of = (jnp.einsum('bkgcqm,bmkd->bcqkgd', p[..., :N_META], vm)
          + jnp.einsum('bkgcqs,bcskd->bcqkgd', p[..., N_META:N_META + NB], vb))
    of = of.reshape(B, n_frames, ATT_Q)

    sm = jnp.einsum('bqkgd,bmkd->bkgqm', qm, km).astype(jnp.float32) * scale
    sm_sink = jnp.broadcast_to(sink[None, :, :, None, None], (B, ATT_KV_HEADS, G, N_META, 1))
    pm = jax.nn.softmax(jnp.concatenate([sm, sm_sink], axis=-1), axis=-1).astype(v.dtype)
    om = jnp.einsum('bkgqm,bmkd->bqkgd', pm[..., :N_META], vm).reshape(B, N_META, ATT_Q)
    return jnp.concatenate([om, of], axis=1)

def gated_linear_attention(q, k, v, log_a):
    B, L = q.shape[0], q.shape[1]
    lead = (-L) % CHUNK
    nc = (L + lead) // CHUNK

    def chunked(t):
        t = jnp.pad(t.astype(jnp.float32), ((0, 0), (lead, 0), (0, 0), (0, 0)))
        return t.reshape(B, nc, CHUNK, t.shape[2], t.shape[3]).transpose(0, 3, 1, 2, 4)

    qc = chunked(q) * (GLA_DK ** -0.5)
    kc, vc, gc = chunked(k), chunked(v), chunked(log_a)
    b = jnp.cumsum(gc, axis=3)
    qe = qc * jnp.exp(b)
    ke = kc * jnp.exp(-b)
    causal = jnp.tril(jnp.ones((CHUNK, CHUNK), dtype=bool))
    att = jnp.where(causal, jnp.einsum('bhcid,bhcjd->bhcij', qe, ke), 0.0)
    o_intra = jnp.einsum('bhcij,bhcjv->bhciv', att, vc)

    b_last = b[:, :, :, -1:]
    chunk_kv = jnp.einsum('bhcjd,bhcjv->bhcdv', kc * jnp.exp(b_last - b), vc)
    decay = jnp.exp(b_last[:, :, :, 0])

    def step(S, inp):
        dec, kv = inp
        return dec[..., None] * S + kv, S

    S0 = jnp.zeros((B, q.shape[2], GLA_DK, GLA_DV), jnp.float32)
    _, S_start = lax.scan(step, S0, (jnp.moveaxis(decay, 2, 0), jnp.moveaxis(chunk_kv, 2, 0)))
    S_start = jnp.moveaxis(S_start, 0, 2)
    o_inter = jnp.einsum('bhcid,bhcdv->bhciv', qe, S_start)
    o = (o_intra + o_inter).transpose(0, 2, 3, 1, 4).reshape(B, nc * CHUNK, q.shape[2], GLA_DV)
    return o[:, lead:]

def second_inputs(seed: int = 0) -> dict:
    key = jax.random.key(seed)
    ks = jax.random.split(key, 24)
    f32 = jnp.float32

    def nrm(k, shape, scale):
        return jax.random.normal(k, shape, f32) * scale

    def gain(k, shape):
        return 1.0 + 0.02 * jax.random.normal(k, shape, f32)

    return {
        "x": nrm(ks[0], (BATCH, SEQ, D_MODEL), 1.0),
        "meta_tokens": nrm(ks[1], (N_META, D_MODEL), 1.0),
        "ffn1_norm": gain(ks[2], (DEPTH, D_MODEL)),
        "ffn1_w_gate": nrm(ks[3], (DEPTH, D_MODEL, D_FF), D_MODEL ** -0.5),
        "ffn1_w_up": nrm(ks[4], (DEPTH, D_MODEL, D_FF), D_MODEL ** -0.5),
        "ffn1_w_down": nrm(ks[5], (DEPTH, D_FF, D_MODEL), D_FF ** -0.5),
        "mix_norm": gain(ks[6], (DEPTH, D_MODEL)),
        "w_in": nrm(ks[7], (DEPTH, D_MODEL, D_IN), D_MODEL ** -0.5),
        "gla_gate_w": nrm(ks[8], (DEPTH, GLA_GATE_RANK, GLA_QK), GLA_GATE_RANK ** -0.5),
        "gla_gate_b": nrm(ks[9], (DEPTH, GLA_QK), 0.1),
        "gla_out_norm": gain(ks[10], (DEPTH, GLA_DV)),
        "att_sinks": nrm(ks[11], (DEPTH, ATT_HEADS), 1.0),
        "w_branch_att": nrm(ks[12], (DEPTH, ATT_Q, D_MODEL), ATT_Q ** -0.5),
        "w_branch_gla": nrm(ks[13], (DEPTH, GLA_V, D_MODEL), GLA_V ** -0.5),
        "w_out": nrm(ks[14], (DEPTH, D_MODEL, D_MODEL), D_MODEL ** -0.5),
        "ffn2_norm": gain(ks[15], (DEPTH, D_MODEL)),
        "ffn2_w_gate": nrm(ks[16], (DEPTH, D_MODEL, D_FF), D_MODEL ** -0.5),
        "ffn2_w_up": nrm(ks[17], (DEPTH, D_MODEL, D_FF), D_MODEL ** -0.5),
        "ffn2_w_down": nrm(ks[18], (DEPTH, D_FF, D_MODEL), D_FF ** -0.5),
        "final_norm": gain(ks[19], (D_MODEL,)),
    }

def second_block(x, meta_tokens, ffn1_norm, ffn1_w_gate, ffn1_w_up, ffn1_w_down, mix_norm, w_in,
              gla_gate_w, gla_gate_b, gla_out_norm, att_sinks, w_branch_att, w_branch_gla, w_out,
              ffn2_norm, ffn2_w_gate, ffn2_w_up, ffn2_w_down, final_norm):
    B = x.shape[0]
    meta = jnp.broadcast_to(meta_tokens[None].astype(x.dtype), (B, N_META, D_MODEL))
    h = jnp.concatenate([meta, x], axis=1)
    L = h.shape[1]
    offsets = np.cumsum(SPLITS)[:-1]
    for l in range(DEPTH):
        h = h + 0.5 * swiglu(rmsnorm(h, ffn1_norm[l]), ffn1_w_gate[l], ffn1_w_up[l], ffn1_w_down[l])

        u = rmsnorm(h, mix_norm[l])
        (aq, ak, av, gq, gk, gv, gr, g_low, gate_a, gate_b) = jnp.split(u @ w_in[l], offsets, axis=-1)

        ya = window_sink_attention(aq.reshape(B, L, ATT_HEADS, ATT_HEAD_DIM),
                                   ak.reshape(B, L, ATT_KV_HEADS, ATT_HEAD_DIM),
                                   av.reshape(B, L, ATT_KV_HEADS, ATT_HEAD_DIM),
                                   att_sinks[l])

        z = (g_low @ gla_gate_w[l] + gla_gate_b[l]).astype(jnp.float32)
        log_a = jax.nn.log_sigmoid(z) / GLA_GATE_TEMP
        og = gated_linear_attention(gq.reshape(B, L, GLA_HEADS, GLA_DK),
                                    gk.reshape(B, L, GLA_HEADS, GLA_DK),
                                    gv.reshape(B, L, GLA_HEADS, GLA_DV),
                                    log_a.reshape(B, L, GLA_HEADS, GLA_DK)).astype(x.dtype)
        og = rmsnorm(og, gla_out_norm[l]) * jax.nn.silu(gr.reshape(B, L, GLA_HEADS, GLA_DV))
        yb = og.reshape(B, L, GLA_V)

        mixed = (jax.nn.sigmoid(gate_a) * (ya @ w_branch_att[l])
                 + jax.nn.sigmoid(gate_b) * (yb @ w_branch_gla[l]))
        h = h + mixed @ w_out[l]

        h = h + 0.5 * swiglu(rmsnorm(h, ffn2_norm[l]), ffn2_w_gate[l], ffn2_w_up[l], ffn2_w_down[l])
    return rmsnorm(h, final_norm)[:, N_META:]


def setup_inputs(seed=0):
    out = dict(first_inputs(seed))
    for name, value in second_inputs(seed + 1).items():
        if name != "x":
            out[name + "_2"] = value
    return out


def reference(
    x, c, w_in, b_f, rel_bias, w_br_fox, w_br_chunk, w_out, w_up, conv_w, conv_b, w_down, w_ada,
    b_ada, ln1_g, ln1_b, ln2_g, ln2_b, meta_tokens_2, ffn1_norm_2, ffn1_w_gate_2, ffn1_w_up_2,
    ffn1_w_down_2, mix_norm_2, w_in_2, gla_gate_w_2, gla_gate_b_2, gla_out_norm_2, att_sinks_2,
    w_branch_att_2, w_branch_gla_2, w_out_2, ffn2_norm_2, ffn2_w_gate_2, ffn2_w_up_2,
    ffn2_w_down_2, final_norm_2,
):
    x = first_block(
        x, c, w_in, b_f, rel_bias, w_br_fox, w_br_chunk, w_out, w_up, conv_w, conv_b, w_down,
        w_ada, b_ada, ln1_g, ln1_b, ln2_g, ln2_b,
    )
    return second_block(
        x, meta_tokens_2, ffn1_norm_2, ffn1_w_gate_2, ffn1_w_up_2, ffn1_w_down_2, mix_norm_2,
        w_in_2, gla_gate_w_2, gla_gate_b_2, gla_out_norm_2, att_sinks_2, w_branch_att_2,
        w_branch_gla_2, w_out_2, ffn2_norm_2, ffn2_w_gate_2, ffn2_w_up_2, ffn2_w_down_2,
        final_norm_2,
    )


_drawn_inputs = setup_inputs


def setup_inputs(seed=0):
    import zlib

    import numpy as np

    out = dict(_drawn_inputs(seed))
    spreads = {}
    factors = {'rel_bias': 4.532,
     'conv_b': 8.0,
     'b_ada': 5.327,
     'ln1_b': 4.207,
     'ln2_b': 4.463,
     'ffn1_norm_2': 5.965,
     'mix_norm_2': 4.459,
     'gla_gate_b_2': 4.647,
     'gla_out_norm_2': 23.419,
     'att_sinks_2': 64.0,
     'ffn2_norm_2': 21.76}
    for name, (base, spread) in spreads.items():
        noise = np.random.default_rng([zlib.crc32(name.encode()), seed]).standard_normal(out[name].shape)
        drawn = base * np.exp(spread * noise) if base else spread * noise
        out[name] = __import__('jax').numpy.asarray(drawn.astype(out[name].dtype))
    for name, factor in factors.items():
        out[name] = (out[name] * factor).astype(out[name].dtype)
    return out
```

```python
from contextlib import ExitStack

import concourse.bass as bass
from concourse import mybir

FP32 = mybir.dt.float32
F32R = mybir.dt.float32r
BF16 = mybir.dt.bfloat16
ACT = mybir.ActivationFunctionType
ALU = mybir.AluOpType
AX = mybir.AxisListType

P = 128
D = 1024
KT = D // P
SEQ = 512
META = 16
TOK = SEQ + META
HALF = TOK // 2
NB = SEQ // P
HEAD = 64
HEADS = 8
CHUNK = 64
D_FF = 2816
FT = D_FF // P
FH = FT // 2
GLA_HEADS = 4
GLA_CHUNKS = SEQ // CHUNK
RANK = 16
ADA = 6 * KT
ADA_FIRST = 2 * KT
ADA_STEP = 3
ALPHA = 2.0 ** 0.25
LN_EPS = 1e-5
RMS_EPS = 1e-6
NEG = -1e30
WC = KT * 2 * P
WF = KT // 2 * P
WG = KT * P
WD = FH * P
QSCALE = HEAD ** -0.5

VECS = [("c", KT), ("b_ada", 48), ("conv_w", 3 * 2 * FT), ("conv_b", 2 * FT), ("ln1_g", KT), ("ln1_b", KT),
        ("ln2_g", KT), ("ln2_b", KT), ("ffn1_norm", KT), ("mix_norm", KT), ("ffn2_norm", KT),
        ("final_norm", KT), ("gla_gate_b", 2), ("gla_out_norm", 1), ("sinks", HEADS), ("b_f", 1)]
VEC_AT = {name: sum(w for _, w in VECS[:i]) for i, (name, _) in enumerate(VECS)}
VEC_COLS = sum(w for _, w in VECS)

STAGES = [("fox", [WC] * 6 + [WF] * 2, 7), ("band", [WC] * 6, 6), ("merge1", [WC] * 12, 12),
          ("out1", [WC] * 4, 4), ("up1", [WC] * FT, FT), ("down1", [WD] * 2 * KT, KT),
          ("up2", [WC] * FT, FT), ("down2", [WD] * 2 * KT, KT), ("win", [WC] * 3 + [WG], 5),
          ("gla", [WC] * 6, 6), ("merge2", [WC] * 12, 12), ("out2", [WC] * 4, 4),
          ("up3", [WC] * FT, FT), ("down3", [WD] * 2 * KT, KT)]


class Stage:

    def __init__(self, chunk, array_index, words, held, n_batches):
        self.c, self.at, self.words, self.held, self.n = chunk, array_index, words, held, n_batches


def plan():
    stages, c, held, seen = {}, 0, [0, 0], {}
    for name, words, nb in STAGES:
        stages[name] = Stage(c, seen.get(words[0], 0), words, tuple(held), nb)
        for w in words:
            seen[w] = seen.get(w, 0) + 1
        c += len(words)
        held[0] += (nb + 1) // 2
        held[1] += nb // 2
    return stages, [w for _, ws, _ in STAGES for w in ws]



class At:

    def __init__(self, base, step=0, i=0):
        self.base, self.step, self.i = base, step, i

    def __add__(self, k):
        return At(self.base + k, self.step, self.i)

    @property
    def n(self):
        return self.step * self.i + self.base if self.step else self.base

    @property
    def half(self):
        return (self.step // 2) * self.i + self.base // 2 if self.step else self.base // 2

    @property
    def odd(self):
        return self.base % 2


def build_program(nc, wts, wfg, wlow, wdown, wada, vecs, xT, metaT, gate_w, band_rel, cf, cb, cw, cs, out):
    st, words = plan()
    n_chunks = len(words)
    with ExitStack() as ctx:
        def sb(name, shape, dt, scope=ctx):
            return scope.enter_context(nc.sbuf_tensor(name, shape, dt))

        sems = {}

        def sem(name):
            if name not in sems:
                sems[name] = ctx.enter_context(nc.semaphore(name))
            return sems[name]

        W_raw = sb("W_raw", [P, 2, WC], FP32)
        W_hi = sb("W_hi", [P, 2, WC], F32R)
        W_lo = sb("W_lo", [P, 2, WC], F32R)
        X = sb("X", [P, KT, TOK], FP32)
        H_hi = sb("H_hi", [P, KT, TOK], F32R)
        with ExitStack() as over:
            SQ = sb("SQ", [P, KT, TOK], FP32, over)
        H_lo = sb("H_lo", [P, KT, TOK], F32R)
        T = sb("T", [P, 3 * 2 * TOK], FP32)
        V = sb("V", [P, VEC_COLS], FP32)
        CF = sb("CF", [P, 3 * P], FP32)
        CB = sb("CB", [P, 2 * P], BF16)
        mod = sb("mod", [P, ADA], FP32)
        mod1 = sb("mod1", [P, ADA], FP32)
        silu_c = sb("silu_c", [P, KT], FP32)
        inv_d = sb("inv_d", [P, 1], FP32)
        inv_v = sb("inv_v", [P, 1], FP32)
        one = sb("one", [P, 1], FP32)
        small = sb("small", [P, 4, 16], FP32)
        stat = sb("stat", [P, 6, HEADS * NB], FP32)
        A_ring = T[:, 0:3 * D].rearrange("p (s w) -> p s w", s=3)
        TA, TB, TC = (T[:, n * 2 * TOK:(n + 1) * 2 * TOK].rearrange("p (m t) -> p m t", m=2) for n in range(3))
        ident, exch, tri = CF[:, 0:P], CF[:, P:2 * P], CF[:, 2 * P:3 * P]
        ident_b, causal_b = CB[:, 0:P], CB[:, P:2 * P]
        with ExitStack() as over:
            G_hi = sb("G_hi", [P, FT, TOK], F32R, over)
            G_lo = sb("G_lo", [P, FT, TOK], F32R, over)
        with ExitStack() as over:
            N1 = sb("N1", [P, KT, TOK], FP32, over)
            N2 = sb("N2", [P, KT, TOK], FP32, over)
        with ExitStack() as over:
            Q = sb("Q", [P, 4, SEQ], FP32, over)
            K = sb("K", [P, 4, SEQ], FP32, over)
            VT = sb("VT", [P, NB, SEQ], FP32, over)
            PR = sb("PR", [P, 3, SEQ], FP32, over)
            PT = sb("PT", [P, 3, SEQ], FP32, over)
            O_hi = sb("O_hi", [P, 8, SEQ], F32R, over)
            O_lo = sb("O_lo", [P, 8, SEQ], F32R, over)
            BAND = sb("BAND", [P, HEADS, 2 * P], FP32, over)
            BAND0 = sb("BAND0", [P, HEADS], FP32, over)
            F = sb("F", [HEADS, 3, SEQ], FP32, over)
        with ExitStack() as over:
            M_hi = sb("M_hi", [P, KT, SEQ], F32R, over)
            M_lo = sb("M_lo", [P, KT, SEQ], F32R, over)
        late = 4 * (5 * 2 * P + 2 * GLA_CHUNKS * P + GLA_HEADS * NB * P + GLA_HEADS * SEQ)
        early = 4 * (4 * SEQ + TOK + (NB + 1) * P + 6 * 3 * P)
        with ExitStack() as over:
            WQ = sb("WQ", [P, 4, SEQ], FP32, over)
            WK = sb("WK", [P, TOK], FP32, over)
            WV = sb("WV", [P, NB + 1, P], FP32, over)
            WPR = sb("WPR", [P, 3, 3 * P], FP32, over)
            WPT = sb("WPT", [P, 3, 3 * P], FP32, over)
            sb("filler", [P, (late - early) // 4], FP32, over)
            LQ = sb("LQ", [P, 2, TOK], FP32, over)
            LK = sb("LK", [P, 2, TOK], FP32, over)
            O2_hi = sb("O2_hi", [P, 8, SEQ], F32R, over)
            O2_lo = sb("O2_lo", [P, 8, SEQ], F32R, over)
            LE = sb("LE", [P, 2, TOK], FP32, over)
            LL = sb("LL", [P, 2, TOK], FP32, over)
            LV = sb("LV", [P, NB + 1, SEQ], FP32, over)
            RESET = sb("RESET", [P, TOK], FP32, over)
            GW = sb("GW", [RANK, 2 * P], FP32, over)
            CW = sb("CW", [P, 2 * P + HEADS * P], BF16, over)
        with ExitStack() as over:
            KL = sb("KL", [P, NB + 1, 2 * P], FP32, over)
            S = sb("S", [P, 2, GLA_CHUNKS, P], FP32, over)
            AM = sb("AM", [P, GLA_HEADS, NB, P], FP32, over)
            OG = sb("OG", [P, GLA_HEADS, SEQ], FP32, over)
        PS = ctx.enter_context(nc.psum_tensor("PS", [P, 8, 512], FP32))

        w_loaded = [sem("w_loaded0"), sem("w_loaded1")]
        w_hi, w_lo = sem("w_hi"), sem("w_lo")
        w_used = sem("w_used")
        psum_free = [sem("psum_free0"), sem("psum_free1")]

        def vec(name, k=0, n=1):
            return V[:, bass.ds(k + VEC_AT[name], n)]

        def free_at(s, b):
            return psum_free[b.odd], b.half + s.held[b.odd]

        def pview(b, m, tok):
            bank = 4 * b.odd + 2 * m
            return PS[:, bank:bank + 1, :] if tok == SEQ else PS[:, bank:bank + 2, 0:HALF]

        def halves(tile, tok):
            return tile.rearrange("p (a t) -> p a t", a=1 if tok == SEQ else 2)

        def spans(tok):
            return [(0, SEQ)] if tok == SEQ else [(0, HALF), (HALF, HALF)]


        class Attention:

            def __init__(self, before, heads, width, blocks, probs, turned, o_hi, o_lo, out_at, sinks):
                self.before, self.width, self.blocks, self.sinks = before, width, blocks, sinks
                self.probs, self.turned, self.o_hi, self.o_lo, self.out_at = probs, turned, o_hi, o_lo, out_at
                self.items = [(h, n // 2, n % 2, i) for n, h in enumerate(heads) for i in range(NB)]
                self.n = len(self.items)

            def sem(self, what):
                return sem(f"att_{what}")

            def reach(self, what, value):
                if what in ("key_max", "sink", "total"):
                    return self.sem(what), value
                return self.sem(what), value + self.before * (HEADS // 2 if what in ("out_hi", "out_lo") else HEADS * NB)

        def first_blocks(i):
            return [(P * j, P, j) for j in range(i + 1)]

        def window_blocks(i):
            meta = [(0, META, NB)]
            return meta + ([(META, P, i)] if i == 0 else [(META, P, i - 1), (META + P, P, i)])

        fox = Attention(0, range(HEADS), lambda i: P * (i + 1), first_blocks, PR, PT, O_hi, O_lo, 0, False)
        band = Attention(1, range(HEADS), lambda i: P * (i + 1), first_blocks, PR, PT, O_hi, O_lo, 4, False)
        win = Attention(2, [h for t in range(4) for h in (t, 4 + t)],
                        lambda i: META + P * (1 if i == 0 else 2), window_blocks, WPR, WPT, O2_hi, O2_lo, 0, True)

        class Norm:

            def __init__(self, number, at, tok, center, gain, bias, to, src_ready):
                self.number, self.at, self.tok, self.center = number, at, tok, center
                self.gain, self.bias, self.to, self.src_ready = gain, bias, to, src_ready
                self.bs = P if tok == SEQ else TOK // 6
                self.nb = tok // self.bs
                self.eps = LN_EPS if center else RMS_EPS

            def sem(self, what):
                return sem(f"norm_{what}")

            def count(self, what):
                if what in ("mean_sum", "mean", "mean_spread", "centred") and not self.center:
                    return 0
                if (what == "scaled" and self.to == "N") or (what == "rounded" and self.to != "H"):
                    return 0
                return KT if what in ("centred", "squared", "scaled", "rounded", "done") else 1

            def reach(self, what, value):
                return self.sem(what), value + sum(m.count(what) for m in norms[:self.number])

            def src(self, k):
                return X[:, k, self.at:self.at + self.tok]

            def centred(self, k):
                return N1[:, k, 0:self.tok] if self.center else self.src(k)

            def spread(self, bank):
                return PS[:, bank:bank + 1, :] if self.tok == SEQ else PS[:, bank:bank + 2, 0:HALF]

            def spread_at(self, bank, b):
                if self.tok == SEQ:
                    return PS[:, bank, b * P:(b + 1) * P]
                return PS[:, bank + b // 3, b % 3 * self.bs:(b % 3 + 1) * self.bs]

        MODCOL = {"sh1": 0, "sc1": KT, "g1": 2 * KT, "sh2": 3 * KT, "sc2": 4 * KT, "g2": 5 * KT}

        def modv(name):
            return lambda k: mod[:, MODCOL[name] + k:MODCOL[name] + k + 1]

        def modv1(name):
            return lambda k: mod1[:, MODCOL[name] + k:MODCOL[name] + k + 1]

        def vv(name):
            return lambda k: vec(name, k)

        norms = [
            Norm(0, META, SEQ, True, modv1("sc1"), modv("sh1"), "H", None),
            Norm(1, META, SEQ, True, vv("ln1_g"), vv("ln1_b"), "X", "out1_x"),
            Norm(2, META, SEQ, True, modv1("sc2"), modv("sh2"), "H", 1),
            Norm(3, META, SEQ, True, vv("ln2_g"), vv("ln2_b"), "X", "down1_x"),
            Norm(4, 0, TOK, False, vv("ffn1_norm"), None, "H", 3),
            Norm(5, 0, TOK, False, vv("mix_norm"), None, "H", "down2_x"),
            Norm(6, META, SEQ, False, vv("ffn2_norm"), None, "H", "out2_x"),
            Norm(7, META, SEQ, False, vv("final_norm"), None, "N", "down3_x"),
        ]
        LN_IN, LN_1, LN_MID, LN_2, RMS_1, RMS_MIX, RMS_2, RMS_OUT = norms

        def wait_src(eng, n, k):
            if n.src_ready is None:
                eng.wait_ge(sem("x_loaded"), 16)
            elif isinstance(n.src_ready, int):
                eng.wait_ge(*norms[n.src_ready].reach("done", k + 1))
            else:
                eng.wait_ge(sem(n.src_ready), k + 1)

        def kv_at(m, n):
            if n == 0:
                return PS[:, 3, m * P:(m + 1) * P]
            return PS[:, 4 + 2 * m + (n - 1) % 2, (n - 1) // 2 * P:((n - 1) // 2 + 1) * P]

        def squares(h):
            return T[:, h * SEQ:(h + 1) * SEQ]

        def retire(ins, s, b):
            return ins.then_inc(psum_free[b.odd], 1)

        def walk(eng, split, s, n, per, body):
            end = s.c + n * per
            after = words[end] if end < n_chunks else 0

            def one_round(i, step, size_after):
                for k in range(per):
                    nxt = At(s.c + k + 1, step, i)
                    size = s.words[0] if k < per - 1 else size_after
                    if size:
                        split(nxt, size)
                    body(i, step, k)

            if after == s.words[0]:
                with eng.Fori(0, n) as i:
                    one_round(i, per, after)
            else:
                with eng.Fori(0, n - 1) as i:
                    one_round(i, per, s.words[0])
                one_round(n - 1, per, after)

        block = ctx.enter_context(nc.Block())

        @block.sync
        def _(sp):
            def load(src, c):
                if not (c.step == 0 and c.base < 2):
                    sp.wait_ge(w_lo, (c + -1).n)
                n = src.shape[-1]
                sp.dma_start(W_raw[:, c.odd, 0:n], src).then_inc(w_loaded[c.odd], 16)

            def pick(arr, n):
                return arr[bass.ds(n, 1)].rearrange("o p n -> (o p) n")

            def load_stage(name):
                s = st[name]
                arr = wdown if s.words[0] == WD else wts
                special = {"fox": wfg, "win": wlow}.get(name)
                plain = [w for w in s.words if w == s.words[0]]
                if name in ("fox", "win", "band", "gla") or s.c < 2:
                    for k in range(len(plain)):
                        load(pick(arr, s.at + k), At(s.c + k))
                else:
                    with sp.Fori(0, len(plain) // 2) as i:
                        for k in range(2):
                            load(pick(arr, 2 * i + (s.at + k)), At(s.c + k, 2, i))
                if special is not None:
                    for k in range(len(s.words) - len(plain)):
                        load(pick(special, k), At(s.c + len(plain) + k))

            sp.dma_start(X[:, :, META:TOK], xT).then_inc(sem("x_loaded"), 16)
            for name, _, _ in STAGES:
                load_stage(name)
            for k in range(KT):
                sp.wait_ge(*RMS_OUT.reach("done", k + 1))
                sp.dma_start(out[:, k, :], N2[:, k, 0:SEQ]).then_inc(sem("stored"), 16)
            sp.wait_ge(sem("stored"), 16 * KT)

        @block.gpsimd
        def _(pool):
            def small_load(dst, src, name):
                pool.dma_start(dst, src).then_inc(sem(name), 16)

            small_load(V[:, :], vecs, "vec_loaded")
            small_load(CF[:, :], cf, "const_loaded")
            small_load(CB[:, :], cb, "const_loaded")
            for t in range(3):
                small_load(A_ring[:, t, :], wada[t], f"ada_loaded{t}")
            rows = bass.AP(tensor=band_rel.tensor, offset=0, ap=[[1, P], [3 * P, HEADS], [1, 2 * P]])
            small_load(BAND[:, :, :], rows, "band_loaded")
            small_load(X[:, :, 0:META], metaT, "meta_loaded")
            for t in range(3, ADA):
                pool.wait_ge(sem("ada_used"), t - 2)
                small_load(A_ring[:, t % 3, :], wada[t], f"ada_loaded{t % 3}")
            pool.wait_ge(*RMS_MIX.reach("scaled", 1))
            small_load(RESET[:, :], cs, "mix_const_loaded")
            small_load(CW[:, :], cw, "mix_const_loaded")
            small_load(GW[:, :], gate_w, "mix_const_loaded")
            pool.wait_ge(sem("mix_const_loaded"), 48)

        @block.tensor
        def _(pe):
            def mm(*a, **kw):
                return nc.tensor.matmul(*a, **kw)

            def chunk_ready(c):
                pe.wait_ge(w_lo, (c + 1).n)

            def group_free(s, b):
                sm, v = free_at(s, b)
                if not (isinstance(v, int) and v == 0):
                    pe.wait_ge(sm, v)

            def feature_tile(outs, slot, off, stride, ks, act_hi, act_lo, start=True, stop=True):
                for n, k in enumerate(ks):
                    a = off + n * stride
                    wh, wl = W_hi[:, slot, a:a + P], W_lo[:, slot, a:a + P]
                    for m, (w, x) in enumerate(((wh, act_hi), (wh, act_lo), (wl, act_hi))):
                        for o, (t0, tn) in outs:
                            last = mm(o, w, x[:, k, t0:t0 + tn], start=start and n == 0 and m == 0,
                                      stop=stop and n == len(ks) - 1 and m == 2)
                return last

            def token_tile(o, tok0, slot, off, stride, n_cols):
                for k in range(KT):
                    a = off + k * stride
                    wh, wl = W_hi[:, slot, a:a + n_cols], W_lo[:, slot, a:a + n_cols]
                    xh, xl = H_hi[:, k, tok0:tok0 + P], H_lo[:, k, tok0:tok0 + P]
                    for m, (x, w) in enumerate(((xh, wh), (xh, wl), (xl, wh))):
                        last = mm(o, x, w, start=k == 0 and m == 0, stop=k == KT - 1 and m == 2)
                return last

            def outs_of(b, m, tok, at):
                v = pview(b, m, tok)
                return [(v[:, n, 0:tn], (at + t0, tn)) for n, (t0, tn) in enumerate(spans(tok))]

            def project(s, c, b, tok, at, act_hi=H_hi, act_lo=H_lo, ks=range(KT), tiles=2):
                chunk_ready(c)
                group_free(s, b)
                for m in range(tiles):
                    last = feature_tile(outs_of(b, m, tok, at), c.odd, m * P, tiles * P, ks, act_hi, act_lo)
                last.then_inc(w_used, 1)

            def take_ada(t):
                pe.wait_ge(sem(f"ada_loaded{t % 3}"), 16 * (t // 3 + 1))
                for k in range(KT):
                    last = mm(PS[:, 7, t:t + 1], A_ring[:, t % 3, k * P:(k + 1) * P], silu_c[:, k:k + 1],
                              start=k == 0, stop=k == KT - 1)
                last.then_inc(sem("ada_used"), 1)

            ada_next = [ADA_FIRST]

            def some_ada():
                for _ in range(ADA_STEP):
                    if ada_next[0] < ADA:
                        take_ada(ada_next[0])
                        ada_next[0] += 1

            def statistic(n, tile_of, wait, done):
                for k in range(KT):
                    wait(k)
                    for b in range(n.nb):
                        last = mm(PS[0:n.bs, 0, b:b + 1], tile_of(k)[:, b * n.bs:(b + 1) * n.bs], inv_d[:, 0:1],
                                  start=k == 0 and b == 0, stop=k == KT - 1, skip_group_check=True)
                last.then_inc(done, 1)

            def spread(n, row, bank, ready, done):
                pe.wait_ge(*ready)
                for b in range(n.nb):
                    last = mm(n.spread_at(bank, b), small[0:n.bs, row, b:b + 1].to_broadcast([n.bs, P]),
                              ident[0:n.bs, 0:n.bs], start=True, stop=True)
                last.then_inc(done, 1)

            def norm(n, after):
                for g in range(2):
                    if after[g]:
                        pe.wait_ge(psum_free[g], after[g])
                if n.center:
                    statistic(n, n.src, lambda k: wait_src(pe, n, k), n.sem("mean_sum"))
                    spread(n, 0, 4, n.reach("mean", 1), n.sem("mean_spread"))
                statistic(n, lambda k: SQ[:, k, 0:n.tok], lambda k: pe.wait_ge(*n.reach("squared", k + 1)), n.sem("var_sum"))
                spread(n, 3, 6, n.reach("inverse", 1), n.sem("inverse_spread"))
                if n.to == "H":
                    pe.wait_ge(*n.reach("done", KT))

            def held_before(name):
                return st[name].held

            def attend(a, scores):
                for t in range(a.n + 2):
                    if t < a.n:
                        h, pair, half, i = a.items[t]
                        if t >= 2:
                            pe.wait_ge(*a.reach("prob", t - 1))
                        scores(PS[:, t % 2, :], h, pair, half, i).then_inc(a.sem("scores"), 1)
                    if 1 <= t <= a.n:
                        u = t - 1
                        i = a.items[u][3]
                        pe.wait_ge(*a.reach("normed", u + 1))
                        if u >= 2:
                            pe.wait_ge(*a.reach("copied", u - 1))
                        for n, (col, keys, _) in enumerate(a.blocks(i)):
                            last = nc.tensor.transpose(PS[0:keys, 2 + u % 2, n * P:(n + 1) * P],
                                                       a.probs[:, u % 3, col:col + keys], ident)
                        last.then_inc(a.sem("turned"), 1)
                    if t >= 2:
                        v = t - 2
                        h, pair, half, i = a.items[v]
                        pe.wait_ge(*a.reach("copied", v + 1))
                        if v % (2 * NB) == 0 and pair >= 2:
                            pe.wait_ge(*a.reach("out_lo", pair - 1))
                        o = PS[HEAD * half:HEAD * half + HEAD, 4 + pair % 2, i * P:(i + 1) * P]
                        blocks = a.blocks(i)
                        for n, (_, keys, tile) in enumerate(blocks):
                            values = (WV[0:keys, tile, HEAD * half:HEAD * half + HEAD] if a is win
                                      else VT[0:keys, tile, HEAD * h:HEAD * h + HEAD])
                            last = mm(o, values, a.turned[0:keys, v % 3, n * P:(n + 1) * P],
                                      start=n == 0, stop=n == len(blocks) - 1)
                        last.then_inc(a.sem("pv"), 1)
                pe.wait_ge(*a.reach("prob", a.n))
                pe.wait_ge(*a.reach("copied", a.n))
                pe.wait_ge(*a.reach("out_lo", a.n // (2 * NB)))

            def rows_of(half):
                return slice(HEAD * half, HEAD * half + HEAD)

            def fox_scores(o, h, pair, half, i):
                w = P * (i + 1)
                r = rows_of(half)
                mm(o[:, 0:w], Q[r, pair, i * P:(i + 1) * P], K[r, pair, 0:w], start=True, stop=False)
                mm(o[:, 0:w], ident[0:HEADS, h:h + 1].to_broadcast([HEADS, P]), F[:, 2, 0:w], start=False, stop=True)
                return mm(o[:, i * P:w], ident_b, causal_b, start=False, stop=True, skip_group_check=True)

            def band_scores(o, h, pair, half, i):
                w = P * (i + 1)
                r = rows_of(half)
                mm(o[:, 0:w], Q[r, pair, i * P:(i + 1) * P], K[r, pair, 0:w], start=True, stop=True)
                bias = BAND[:, h, P:2 * P] if i == 0 else BAND[:, h, :]
                return mm(o[:, max(i - 1, 0) * P:w], exch, bias, start=False, stop=True, skip_group_check=True)

            def window_scores(o, h, pair, half, i):
                w = win.width(i)
                r = rows_of(half)
                q = WQ[r, pair, i * P:(i + 1) * P]
                first_key = META + max(i - 1, 0) * P
                distance = CW[:, P:2 * P] if i == 0 else CW[:, 0:2 * P]
                mm(o[:, META:w], q, WK[r, first_key:first_key + w - META], start=True, stop=False)
                mm(o[:, META:w], CW[:, (2 + h) * P:(3 + h) * P], distance, start=False, stop=True)
                return mm(o[:, 0:META], q, WK[r, 0:META], start=False, stop=True, skip_group_check=True)

            def values_fox(s, k):
                c, b = At(s.c + k), At(k)
                chunk_ready(c)
                group_free(s, b)
                for blk in range(NB):
                    last = token_tile(PS[:, 4 * b.odd + blk // 2, blk % 2 * 256:blk % 2 * 256 + 256],
                                      META + blk * P, c.odd, 0, 2 * P, 2 * P)
                last.then_inc(w_used, 1)

            def merge(name, o_hi, o_lo):
                s = st[name]
                with pe.Fori(0, 2) as i:
                    for mp in range(2):
                        for part in range(2):
                            k = 3 * mp + part
                            project(s, At(s.c + k, 6, i), At(k, 6, i), SEQ, META)
                        k = 3 * mp + 2
                        c, b = At(s.c + k, 6, i), At(k, 6, i)
                        chunk_ready(c)
                        group_free(s, b)
                        for m in range(2):
                            for br in range(2):
                                o = PS[:, 4 * b.odd + 2 * m + br, :]
                                last = feature_tile([(o, (0, SEQ))], c.odd, br * 4 * 2 * P + m * P, 2 * P,
                                                    range(4 * br, 4 * br + 4), o_hi, o_lo)
                        last.then_inc(w_used, 1)

            def project_all(name, n, tok, at, act_hi=H_hi, act_lo=H_lo):
                s = st[name]
                with pe.Fori(0, n) as i:
                    for k in range(2):
                        project(s, At(s.c + k, 2, i), At(k, 2, i), tok, at, act_hi, act_lo)

            def down(name, tok, split):
                s = st[name]
                with pe.Fori(0, KT // 2) as i:
                    for b2 in range(2):
                        b = At(b2, 2, i)
                        for half in range(2):
                            c = At(s.c + 2 * b2 + half, 4, i)
                            chunk_ready(c)
                            if half == 0:
                                group_free(s, b)
                            pe.wait_ge(split, (FH - 1) // 2 + 1 if half == 0 else FH)
                            ks = range(FH * half, FH * half + FH)
                            feature_tile(outs_of(b, 0, tok, 0), c.odd, 0, P, ks, G_hi, G_lo,
                                         start=half == 0, stop=half == 1).then_inc(w_used, 1)

            pe.wait_ge(sem("const_loaded"), 32)
            pe.wait_ge(sem("silu_c"), 1)
            pe.wait_ge(sem("consts"), 1)
            for t in range(ADA_FIRST):
                take_ada(t)
            norm(LN_IN, (0, 0))
            s = st["fox"]
            for k in range(2):
                values_fox(s, k)
                some_ada()
            for k in range(2, 6):
                project(s, At(s.c + k), At(k), SEQ, META)
                some_ada()
            for half in range(2):
                c, b = At(s.c + 6 + half), At(6)
                chunk_ready(c)
                if half == 0:
                    group_free(s, b)
                feature_tile(outs_of(b, 0, SEQ, META), c.odd, 0, P, range(4 * half, 4 * half + 4), H_hi, H_lo,
                             start=half == 0, stop=half == 1).then_inc(w_used, 1)
            pe.wait_ge(psum_free[0], st["band"].held[0])
            pe.wait_ge(psum_free[1], st["band"].held[1])
            pe.wait_ge(sem("fox_decay"), 1)
            attend(fox, fox_scores)
            s = st["band"]
            for k in range(2):
                values_fox(s, k)
                some_ada()
            for k in range(2, 6):
                project(s, At(s.c + k), At(k), SEQ, META)
                some_ada()
            assert ada_next[0] == ADA
            pe.wait_ge(psum_free[0], st["merge1"].held[0])
            pe.wait_ge(psum_free[1], st["merge1"].held[1])
            pe.wait_ge(sem("band_bias"), 1)
            attend(band, band_scores)
            pe.wait_ge(sem("mod_rest"), 1)
            merge("merge1", O_hi, O_lo)
            pe.wait_ge(sem("merge1_lo"), 5)
            project_all("out1", 2, SEQ, 0, M_hi, M_lo)
            norm(LN_1, st["up1"].held)
            norm(LN_MID, st["up1"].held)
            project_all("up1", FH, SEQ, META)
            down("down1", SEQ, sem("up1_lo"))
            norm(LN_2, st["up2"].held)
            norm(RMS_1, st["up2"].held)
            project_all("up2", FH, TOK, 0)
            down("down2", TOK, sem("up2_lo"))
            norm(RMS_MIX, st["win"].held)
            s = st["win"]
            for k in range(2):
                project(s, At(s.c + k), At(k), SEQ, META)
            c, b = At(s.c + 2), At(2)
            chunk_ready(c)
            group_free(s, b)
            feature_tile(outs_of(b, 0, TOK, 0), c.odd, 0, 2 * P, range(KT), H_hi, H_lo)
            for blk in range(NB):
                token_tile(PS[:, 4 * b.odd + 2, blk * P:(blk + 1) * P], META + blk * P, c.odd, P, 2 * P, P)
            token_tile(PS[:, 4 * b.odd + 3, 0:P], 0, c.odd, P, 2 * P, P).then_inc(w_used, 1)
            project(s, At(s.c + 3), At(3), TOK, 0, tiles=1)
            b = At(4)
            group_free(s, b)
            pe.wait_ge(psum_free[1], s.held[1] + 2)
            pe.wait_ge(sem("mix_const_loaded"), 48)
            for m in range(2):
                for o, (t0, tn) in outs_of(b, m, TOK, 0):
                    last = mm(o, GW[:, m * P:(m + 1) * P], TC[0:RANK, 0, t0:t0 + tn], start=True, stop=True)
            last.then_inc(sem("z_ready"), 1)
            pe.wait_ge(psum_free[0], st["gla"].held[0])
            pe.wait_ge(psum_free[1], st["gla"].held[1])
            attend(win, window_scores)
            s = st["gla"]
            for k in range(2):
                project(s, At(s.c + k), At(k), TOK, 0)
            for k in range(2, 4):
                c, b = At(s.c + k), At(k)
                chunk_ready(c)
                group_free(s, b)
                for blk in range(NB):
                    token_tile(PS[:, 4 * b.odd + blk // 2, blk % 2 * 256:blk % 2 * 256 + 256],
                               META + blk * P, c.odd, 0, 2 * P, 2 * P)
                token_tile(PS[:, 4 * b.odd + 2, 0:256], 0, c.odd, 0, 2 * P, 2 * P).then_inc(w_used, 1)
            pe.wait_ge(psum_free[0], s.held[0] + 2)
            pe.wait_ge(psum_free[1], s.held[1] + 2)
            for n in range(NB + 1):
                t0 = META + n * P if n < NB else 0
                for m in range(2):
                    last = nc.tensor.transpose(PS[:, n // 2, n % 2 * 256 + m * P:n % 2 * 256 + (m + 1) * P],
                                               LL[:, m, t0:t0 + P], ident)
            last.then_inc(sem("kl_turned"), 1)
            pe.wait_ge(sem("kl_ready"), 1)
            for m in range(2):
                for n in range(GLA_CHUNKS):
                    blk, r = (NB, slice(0, META)) if n == 0 else ((n - 1) // 2, rows_of((n - 1) % 2))
                    for hh in range(2):
                        h = 2 * m + hh
                        last = mm(kv_at(m, n)[rows_of(hh), :],
                                  KL[r, blk, h * HEAD:(h + 1) * HEAD], LV[r, blk, h * P:(h + 1) * P],
                                  start=True, stop=True)
            last.then_inc(sem("kv_ready"), 1)
            for h in range(GLA_HEADS):
                if h == GLA_HEADS - 1:
                    pe.wait_ge(sem("state_ready"), 2)
                for n in range(NB):
                    t0 = META + n * P
                    r = rows_of(h % 2)
                    last = mm(PS[:, h, n * P:(n + 1) * P], LK[r, h // 2, t0:t0 + P], LQ[r, h // 2, t0:t0 + P],
                              start=True, stop=True)
                last.then_inc(sem("att_ready"), 1)
            pe.wait_ge(sem("state_ready"), 2 * GLA_CHUNKS)
            for h in range(GLA_HEADS):
                pe.wait_ge(sem("am_ready"), h + 1)
                for n in range(NB):
                    mm(PS[:, 4 + h, n * P:(n + 1) * P], LV[:, n, h * P:(h + 1) * P], AM[:, h, n, :], start=True, stop=True)
                    for c in (2 * n, 2 * n + 1):
                        r, t0 = rows_of(h % 2), META + c * CHUNK
                        last = mm(PS[:, 4 + h, c * CHUNK:(c + 1) * CHUNK], S[r, h // 2, c, :],
                                  LQ[r, h // 2, t0:t0 + CHUNK], start=False, stop=True, skip_group_check=True)
                last.then_inc(sem("og_raw"), 1)
            for h in range(GLA_HEADS):
                pe.wait_ge(sem("og_squared"), h + 1)
                for n in range(NB):
                    last = mm(PS[:, 0, h * NB + n:h * NB + n + 1], squares(h)[:, n * P:(n + 1) * P], inv_v[:, 0:1],
                              start=True, stop=True)
            last.then_inc(sem("og_sum"), 1)
            pe.wait_ge(sem("og_inverse"), 1)
            for h in range(GLA_HEADS):
                for n in range(NB):
                    last = mm(PS[:, 4 + h, n * P:(n + 1) * P],
                              small[:, 3, h * NB + n:h * NB + n + 1].to_broadcast([P, P]), ident, start=True, stop=True)
            last.then_inc(sem("og_spread"), 1)
            for k in range(4, 6):
                if k == 5:
                    pe.wait_ge(sem("og_normed"), GLA_HEADS)
                project(s, At(s.c + k), At(k), SEQ, META)
            pe.wait_ge(sem("o2_lo"), 2)
            merge("merge2", O2_hi, O2_lo)
            pe.wait_ge(sem("merge2_lo"), 5)
            project_all("out2", 2, SEQ, 0, M_hi, M_lo)
            norm(RMS_2, st["up3"].held)
            project_all("up3", FH, SEQ, META)
            down("down3", SEQ, sem("up3_lo"))
            norm(RMS_OUT, [st["down3"].held[g] + KT // 2 for g in range(2)])
        @block.scalar
        def _(act):
            def activate(*a, **kw):
                return nc.scalar.activation(*a, **kw)

            def split(c, size):
                act.wait_ge(w_loaded[c.odd], (c.half + 1) * 16)
                if not (c.step == 0 and c.base < 2):
                    act.wait_ge(w_used, (c + -1).n)
                activate(W_hi[:, c.odd, 0:size], W_raw[:, c.odd, 0:size], ACT.Copy).then_inc(w_hi, 1)

            def used(c):
                act.wait_ge(w_used, (c + 1).n)

            def norm(n):
                if n.center:
                    for k in range(KT):
                        act.wait_ge(*n.reach("centred", k + 1))
                        activate(SQ[:, k, 0:n.tok], n.centred(k), ACT.Square).then_inc(n.sem("squared"), 1)
                else:
                    for k in range(KT):
                        wait_src(act, n, k)
                        if n is RMS_1 and k == 0:
                            act.wait_ge(sem("meta_loaded"), 16)
                        activate(SQ[:, k, 0:n.tok], n.src(k), ACT.Square).then_inc(n.sem("squared"), 1)
                act.wait_ge(*n.reach("variance", 1))
                activate(small[0:n.bs, 2, 0:n.nb], small[0:n.bs, 1, 0:n.nb], ACT.Sqrt).then_inc(n.sem("deviation"), 1)
                if n.to == "N":
                    return
                for k in range(KT):
                    act.wait_ge(*n.reach("scaled", k + 1))
                    dst = H_hi[:, k, n.at:n.at + n.tok] if n.to == "H" else n.src(k)
                    if n.bias is None:
                        ins = activate(dst, N2[:, k, 0:n.tok], ACT.Copy)
                    else:
                        ins = activate(dst, N2[:, k, 0:n.tok], ACT.Identity, bias=n.bias(k))
                    ins.then_inc(n.sem("rounded" if n.to == "H" else "done"), 1)

            def attend(a):
                def put_out(pair):
                    act.wait_ge(*a.reach("pv", 2 * NB * (pair + 1)))
                    activate(a.o_hi[:, a.out_at + pair, :], PS[:, 4 + pair % 2, :], ACT.Copy).then_inc(a.sem("out_hi"), 1)

                for t in range(a.n + 1):
                    if t < a.n:
                        h, pair, half, i = a.items[t]
                        act.wait_ge(*a.reach("max", t + 1))
                        if t >= 3:
                            act.wait_ge(*a.reach("turned", t - 2))
                        w = a.width(i)
                        activate(a.probs[:, t % 3, 0:w], PS[:, t % 2, 0:w], ACT.Exp, bias=stat[:, 0, t:t + 1],
                                 accum_out=stat[:, 1, t:t + 1]).then_inc(a.sem("prob"), 1)
                        if a.sinks:
                            activate(stat[:, 4, t:t + 1], vec("sinks", h), ACT.Exp,
                                     bias=stat[:, 0, t:t + 1]).then_inc(a.sem("sink"), 1)
                    if t >= 1:
                        u = t - 1
                        act.wait_ge(*a.reach("turned", u + 1))
                        if u >= 3:
                            act.wait_ge(*a.reach("pv", u - 2))
                        n = 0
                        for n, (_, keys, _) in enumerate(a.blocks(a.items[u][3])):
                            if keys < P:
                                activate(a.turned[0:keys, u % 3, n * P:(n + 1) * P],
                                         PS[0:keys, 2 + u % 2, n * P:(n + 1) * P], ACT.Copy)
                        n0 = 1 if a.blocks(0)[0][1] < P else 0
                        activate(a.turned[:, u % 3, n0 * P:(n + 1) * P], PS[:, 2 + u % 2, n0 * P:(n + 1) * P],
                                 ACT.Copy).then_inc(a.sem("copied"), 1)
                        if t % (2 * NB) == 3 and t > 2 * NB:
                            put_out(t // (2 * NB) - 1)
                put_out(a.n // (2 * NB) - 1)

            def copies(s, k, plan_of):
                split(At(s.c + k + 1), words[s.c + k + 1])
                used(At(s.c + k))
                for dst, src, scale in plan_of[:-1]:
                    activate(dst, src, ACT.Copy, scale=scale)
                dst, src, scale = plan_of[-1]
                retire(activate(dst, src, ACT.Copy, scale=scale), s, At(k))

            def value_plan(k, dst, meta=False):
                g = 4 * (k % 2)
                col = 256 * (k % 2)
                p = [(dst[:, 2 * bb:2 * bb + 2, col:col + 256], PS[:, g + bb, :].rearrange("p (b n) -> p b n", b=2), 1.0)
                     for bb in range(2)]
                if meta:
                    p.append((dst[0:META, NB, col:col + 256], PS[0:META, g + 2, 0:256], 1.0))
                return p

            def tile_plan(k, dst, first, scale):
                g = 4 * (k % 2)
                return [(dst[:, first + m, :], PS[:, g + 2 * m, :], scale) for m in range(2)]

            def merge(name, m_hi):
                s = st[name]

                def body(i, step, k):
                    mp, part = k // 3, k % 3
                    c, b = At(s.c + k, step, i), At(k, step, i)
                    rnd = mp + 2 * i
                    if part < 2:
                        used(c)
                        if part == 0:
                            act.wait_ge(sem(f"{name}_lo"), rnd + 1)
                        dst = (TA, TB)[part]
                        for m in range(2):
                            ins = activate(dst[:, m, 0:SEQ], PS[:, 4 * b.odd + 2 * m, :], ACT.Sigmoid)
                        retire(ins, s, b)
                    else:
                        act.wait_ge(sem(f"{name}_sum"), rnd + 1)
                        activate(m_hi[:, bass.ds(2 * rnd, 2), :], TC[:, :, 0:SEQ], ACT.Copy).then_inc(sem(f"{name}_hi"), 1)

                walk(act, split, s, 2, 6, body)

            def up_first(name):
                s = st[name]

                def body(i, step, k):
                    c, b = At(s.c + k, step, i), At(k, step, i)
                    if k == 1:
                        act.wait_ge(psum_free[0], i + (s.held[0] + 1))
                        activate(TA[:, :, 0:SEQ], TA[:, :, 0:SEQ], ACT.Silu).then_inc(sem(f"{name}_silu"), 1)
                    used(c)
                    if k == 0:
                        act.wait_ge(sem(f"{name}_prod"), i + 1)
                    for m in range(2):
                        col = i * 2 + (k * FT + m)
                        activate((TA, TB)[k][:, m, 0:SEQ], PS[:, 4 * b.odd + 2 * m, :], ACT.Identity,
                                 bias=vec("conv_b", col), scale=vec("conv_w", col + 2 * 2 * FT)
                                 ).then_inc(sem(f"{name}_tap"), 1)
                    if k == 1:
                        act.wait_ge(sem(f"{name}_prod"), i + 2)
                        activate(G_hi[:, bass.ds(i * 2, 2), 0:SEQ], TC[:, :, 0:SEQ], ACT.Copy).then_inc(sem(f"{name}_hi"), 1)

                walk(act, split, s, FH, 2, body)

            def up_second(name, tok):
                s = st[name]

                def body(i, step, k):
                    c, b = At(s.c + k, step, i), At(k, step, i)
                    if k == 0:
                        used(c)
                        act.wait_ge(psum_free[1], i + s.held[1])
                        for m in range(2):
                            ins = activate(halves(TA[:, m, 0:tok], tok), pview(b, m, tok), ACT.Silu)
                        retire(ins, s, b)
                    else:
                        act.wait_ge(psum_free[1], i + (s.held[1] + 1))
                        activate(G_hi[:, bass.ds(i * 2, 2), 0:tok], TC[:, :, 0:tok], ACT.Copy).then_inc(sem(f"{name}_hi"), 1)

                walk(act, split, s, FH, 2, body)

            def scale_residual(name, n, per):
                s = st[name]

                def body(i, step, k):
                    if k == 0:
                        activate(X[:, bass.ds(i * (KT // n), KT // n), META:TOK], X[:, bass.ds(i * (KT // n), KT // n), META:TOK],
                                 ACT.Copy, scale=ALPHA).then_inc(sem(f"{name}_alpha"), 1)

                walk(act, split, s, n, per, body)

            def only_split(name, n, per):
                walk(act, split, st[name], n, per, lambda i, step, k: None)

            act.wait_ge(sem("vec_loaded"), 16)
            activate(silu_c[:, :], vec("c", 0, KT), ACT.Silu).then_inc(sem("silu_c"), 1)
            split(At(0), words[0])
            norm(LN_IN)
            s = st["fox"]
            for k in range(2):
                copies(s, k, value_plan(k, VT))
            for k in range(2, 4):
                copies(s, k, tile_plan(k, Q, 2 * (k - 2), QSCALE))
            for k in range(4, 6):
                copies(s, k, tile_plan(k, K, 2 * (k - 4), 1.0))
            split(At(s.c + 7), words[s.c + 7])
            split(At(s.c + 8), words[s.c + 8])
            used(At(s.c + 7))
            retire(activate(F[:, 0, :], PS[0:HEADS, 0, :], ACT.Identity, bias=V[0:HEADS, VEC_AT["b_f"]:VEC_AT["b_f"] + 1]),
                   s, At(6))
            act.wait_ge(sem("fox_abs"), 1)
            activate(F[:, 1, :], F[:, 1, :], ACT.Exp, scale=-1.0).then_inc(sem("fox_exp"), 1)
            act.wait_ge(sem("fox_exp"), 1)
            activate(F[:, 1, :], F[:, 1, :], ACT.Ln, bias=one[0:HEADS, :]).then_inc(sem("fox_log"), 1)
            attend(fox)
            s = st["band"]
            for k in range(2):
                copies(s, k, value_plan(k, VT))
            for k in range(2, 4):
                copies(s, k, tile_plan(k, Q, 2 * (k - 2), QSCALE))
            for k in range(4, 6):
                copies(s, k, tile_plan(k, K, 2 * (k - 4), 1.0))
            attend(band)
            act.wait_ge(sem("ada_used"), ADA)
            merge("merge1", M_hi)
            scale_residual("out1", 2, 2)
            norm(LN_1)
            norm(LN_MID)
            up_first("up1")
            scale_residual("down1", 4, 4)
            norm(LN_2)
            norm(RMS_1)
            up_second("up2", TOK)
            only_split("down2", 4, 4)
            norm(RMS_MIX)
            s = st["win"]
            for k in range(2):
                copies(s, k, tile_plan(k, WQ, 2 * k, QSCALE))
            copies(s, 2, [(halves(WK[:, :], TOK), PS[:, 0:2, 0:HALF], 1.0),
                          (WV[:, 0:NB, :], PS[:, 2, :].rearrange("p (b n) -> p b n", b=NB), 1.0),
                          (WV[0:META, NB, :], PS[0:META, 3, 0:P], 1.0)])
            k = 3
            split(At(s.c + k + 1), words[s.c + k + 1])
            used(At(s.c + k))
            retire(activate(halves(TC[0:RANK, 0, :], TOK), PS[0:RANK, 4:6, 0:HALF], ACT.Copy), s, At(3))
            act.wait_ge(sem("z_ready"), 1)
            for m in range(2):
                ins = activate(halves(TA[:, m, :], TOK), PS[:, 2 * m:2 * m + 2, 0:HALF], ACT.Identity,
                               bias=vec("gla_gate_b", m))
            retire(ins, s, At(4))
            act.wait_ge(sem("z_abs"), 1)
            activate(TB[:, :, :], TB[:, :, :], ACT.Exp, scale=-1.0).then_inc(sem("z_exp"), 1)
            act.wait_ge(sem("z_exp"), 1)
            activate(TB[:, :, :], TB[:, :, :], ACT.Ln, bias=one[:, :]).then_inc(sem("z_log"), 1)
            act.wait_ge(sem("b_ready"), 1)
            activate(TB[:, :, :], LE[:, :, :], ACT.Exp, scale=-1.0 / 16.0)
            activate(LL[:, :, :], LL[:, :, :], ACT.Exp, scale=1.0 / 16.0)
            activate(LE[:, :, :], LE[:, :, :], ACT.Exp, scale=1.0 / 16.0).then_inc(sem("decays"), 1)
            attend(win)
            s = st["gla"]
            for k in range(2):
                split(At(s.c + k + 1), words[s.c + k + 1])
            for k in range(2, 4):
                copies(s, k, value_plan(k, LV, meta=True))
            act.wait_ge(sem("kl_turned"), 1)
            for n in range(0, NB + 1, 2):
                w = 2 if n < NB else 1
                ins = activate(KL[:, n:n + w, :], PS[:, n // 2, 0:w * 256].rearrange("p (b n) -> p b n", b=w), ACT.Copy)
            ins.then_inc(sem("kl_ready"), 1)
            for h in range(GLA_HEADS):
                act.wait_ge(sem("og_raw"), h + 1)
                activate(OG[:, h, :], PS[:, 4 + h, :], ACT.Copy)
                activate(squares(h), PS[:, 4 + h, :], ACT.Square).then_inc(sem("og_squared"), 1)
            act.wait_ge(sem("og_variance"), 1)
            activate(small[:, 2, :], small[:, 1, :], ACT.Sqrt).then_inc(sem("og_deviation"), 1)
            for k in range(4, 6):
                split(At(s.c + k + 1), words[s.c + k + 1])
                used(At(s.c + k))
                if k == 5:
                    act.wait_ge(sem("og_gated"), 1)
                for m in range(2):
                    ins = activate(TA[:, m, 0:SEQ], PS[:, 4 * (k % 2) + 2 * m, :], ACT.Silu)
                retire(ins, s, At(k))
                act.wait_ge(sem("og_gated"), k - 3)
                activate(O2_hi[:, 2 * k - 4:2 * k - 2, :], TB[:, :, 0:SEQ], ACT.Copy).then_inc(sem("o2_hi"), 1)
            merge("merge2", M_hi)
            only_split("out2", 2, 2)
            norm(RMS_2)
            up_second("up3", SEQ)
            only_split("down3", 4, 4)
            norm(RMS_OUT)

        @block.vector
        def _(dve):
            vector = nc.vector

            def split(c, size):
                dve.wait_ge(w_hi, (c + 1).n)
                vector.tensor_tensor(W_lo[:, c.odd, 0:size], W_raw[:, c.odd, 0:size],
                                     W_hi[:, c.odd, 0:size].bitcast(FP32), ALU.subtract).then_inc(w_lo, 1)

            def used(c):
                dve.wait_ge(w_used, (c + 1).n)

            def norm(n):
                if n.center:
                    dve.wait_ge(*n.reach("mean_sum", 1))
                    vector.tensor_copy(small[0:n.bs, 0, 0:n.nb], PS[0:n.bs, 0, 0:n.nb]).then_inc(n.sem("mean"), 1)
                    dve.wait_ge(*n.reach("mean_spread", 1))
                    for k in range(KT):
                        vector.tensor_tensor(halves(n.centred(k), n.tok), halves(n.src(k), n.tok), n.spread(4),
                                             ALU.subtract).then_inc(n.sem("centred"), 1)
                dve.wait_ge(*n.reach("var_sum", 1))
                vector.tensor_scalar(small[0:n.bs, 1, 0:n.nb], PS[0:n.bs, 0, 0:n.nb], n.eps, None, ALU.add
                                     ).then_inc(n.sem("variance"), 1)
                dve.wait_ge(*n.reach("deviation", 1))
                vector.reciprocal(small[0:n.bs, 3, 0:n.nb], small[0:n.bs, 2, 0:n.nb]).then_inc(n.sem("inverse"), 1)
                dve.wait_ge(*n.reach("inverse_spread", 1))

                def leave(k):
                    dve.wait_ge(*n.reach("rounded", k + 1))
                    hi = H_hi[:, k, n.at:n.at + n.tok].bitcast(FP32)
                    lo = H_lo[:, k, n.at:n.at + n.tok]
                    if n.bias is None:
                        ins = vector.tensor_tensor(lo, N2[:, k, 0:n.tok], hi, ALU.subtract)
                    else:
                        ins = vector.scalar_tensor_tensor(out=lo, in0=N2[:, k, 0:n.tok], scalar=n.bias(k), in1=hi,
                                                          op0=ALU.add, op1=ALU.subtract)
                    ins.then_inc(n.sem("done"), 1)

                for k in range(KT):
                    vector.scalar_tensor_tensor(out=halves(N2[:, k, 0:n.tok], n.tok), in0=halves(n.centred(k), n.tok),
                                                scalar=n.gain(k), in1=n.spread(6), op0=ALU.mult, op1=ALU.mult
                                                ).then_inc(n.sem("done" if n.to == "N" else "scaled"), 1)
                    if n.to == "H" and k:
                        leave(k - 1)
                if n.to == "H":
                    leave(KT - 1)

            def attend(a):
                def put_out(pair):
                    dve.wait_ge(*a.reach("out_hi", pair + 1))
                    at = a.out_at + pair
                    vector.tensor_tensor(a.o_lo[:, at, :], PS[:, 4 + pair % 2, :], a.o_hi[:, at, :].bitcast(FP32),
                                         ALU.subtract).then_inc(a.sem("out_lo"), 1)

                for t in range(a.n + 1):
                    if t < a.n:
                        h, pair, half, i = a.items[t]
                        dve.wait_ge(*a.reach("scores", t + 1))
                        w = a.width(i)
                        if a.sinks:
                            vector.tensor_reduce(stat[:, 3, t:t + 1], PS[:, t % 2, 0:w], AX.X, ALU.max
                                                 ).then_inc(a.sem("key_max"), 1)
                            dve.wait_ge(*a.reach("key_max", t + 1))
                            vector.tensor_scalar(stat[:, 0, t:t + 1], stat[:, 3, t:t + 1], vec("sinks", h), -1.0,
                                                 ALU.max, ALU.mult).then_inc(a.sem("max"), 1)
                        else:
                            vector.tensor_reduce(stat[:, 0, t:t + 1], PS[:, t % 2, 0:w], AX.X, ALU.max, negate=True
                                                 ).then_inc(a.sem("max"), 1)
                    if t >= 1:
                        u = t - 1
                        w = a.width(a.items[u][3])
                        total = stat[:, 1, u:u + 1]
                        if a.sinks:
                            dve.wait_ge(*a.reach("sink", u + 1))
                            total = stat[:, 5, u:u + 1]
                            vector.tensor_tensor(total, stat[:, 1, u:u + 1], stat[:, 4, u:u + 1], ALU.add
                                                 ).then_inc(a.sem("total"), 1)
                            dve.wait_ge(*a.reach("total", u + 1))
                        dve.wait_ge(*a.reach("prob", u + 1))
                        vector.reciprocal(stat[:, 2, u:u + 1], total).then_inc(a.sem("inverse"), 1)
                        dve.wait_ge(*a.reach("inverse", u + 1))
                        vector.tensor_scalar(a.probs[:, u % 3, 0:w], a.probs[:, u % 3, 0:w], stat[:, 2, u:u + 1], None,
                                             ALU.mult).then_inc(a.sem("normed"), 1)
                        if t % (2 * NB) == 4 and t > 2 * NB:
                            put_out(t // (2 * NB) - 1)
                put_out(a.n // (2 * NB) - 1)

            def splits(s, n):
                for k in range(n):
                    split(At(s.c + k + 1), words[s.c + k + 1])

            def merge(name, m_hi, m_lo):
                s = st[name]
                dve.sem_inc(sem(f"{name}_lo"), 1)

                def body(i, step, k):
                    mp, part = k // 3, k % 3
                    if part < 2:
                        return
                    c, b = At(s.c + k, step, i), At(k, step, i)
                    rnd = mp + 2 * i
                    used(c)
                    dve.wait_ge(psum_free[1 - b.odd], (At(k - 1, step, i).half + s.held[1 - b.odd]) + 1)
                    for m in range(2):
                        for br in range(2):
                            tile = (TA, TB)[br][:, m, 0:SEQ]
                            ins = vector.tensor_tensor(tile, tile, PS[:, 4 * b.odd + 2 * m + br, :], ALU.mult)
                            if m == 1 and br == 1:
                                retire(ins, s, b)
                    dve.wait_ge(psum_free[b.odd], (b.half + s.held[b.odd]) + 1)
                    vector.tensor_tensor(TC[:, :, 0:SEQ], TA[:, :, 0:SEQ], TB[:, :, 0:SEQ], ALU.add
                                         ).then_inc(sem(f"{name}_sum"), 1)
                    dve.wait_ge(sem(f"{name}_hi"), rnd + 1)
                    vector.tensor_tensor(m_lo[:, bass.ds(2 * rnd, 2), :], TC[:, :, 0:SEQ],
                                         m_hi[:, bass.ds(2 * rnd, 2), :].bitcast(FP32), ALU.subtract
                                         ).then_inc(sem(f"{name}_lo"), 1)

                walk(dve, split, s, 2, 6, body)

            def residual_sum(name, tiles_per_batch, gain, tok, at):
                s = st[name]
                n, per = (2, 2) if tiles_per_batch == 2 else (4, 4)

                def body(i, step, k):
                    if tiles_per_batch == 1 and k % 2 == 0:
                        return
                    b = At(k if tiles_per_batch == 2 else k // 2, 2, i)
                    used(At(s.c + k, step, i))
                    if gain is not None and gain != 0.5 and (k == 0 or (tiles_per_batch == 1 and k == 1)):
                        dve.wait_ge(sem(f"{name}_alpha"), i + 1)
                    for m in range(tiles_per_batch):
                        f = (i * (n_tiles_per_round)) + (m + tiles_per_batch * b.base)
                        x = X[:, bass.ds(f, 1), at:at + tok].rearrange("p o t -> p (o t)")
                        ps = pview(b, m, tok)
                        if gain is None:
                            ins = vector.tensor_tensor(halves(x, tok), ps, halves(x, tok), ALU.add)
                        else:
                            g = 0.5 if gain == 0.5 else mod1[:, bass.ds(f + MODCOL[gain], 1)]
                            ins = vector.scalar_tensor_tensor(out=halves(x, tok), in0=ps, scalar=g, in1=halves(x, tok),
                                                              op0=ALU.mult, op1=ALU.add)
                        ins.then_inc(sem(f"{name}_x"), 1)
                    dve.wait_ge(sem(f"{name}_x"), (i * n_tiles_per_round) + tiles_per_batch * (b.base + 1))
                    dve.sem_inc(psum_free[b.odd], 1)

                n_tiles_per_round = 2 * tiles_per_batch
                walk(dve, split, s, n, per, body)

            def up_first(name):
                s = st[name]
                dve.sem_inc(sem(f"{name}_prod"), 1)

                def body(i, step, k):
                    b = At(k, step, i)
                    tile = (TA, TB)[k]
                    for tap in (1, 2):
                        for m in range(2):
                            if tap == 1:
                                dve.wait_ge(sem(f"{name}_tap"), i * 4 + (2 * k + m + 1))
                            else:
                                dve.wait_ge(sem(f"{name}_near"), i * 4 + (2 * k + m + 1))
                            w = vec("conv_w", i * 2 + (k * FT + m + (2 - tap) * 2 * FT))
                            ins = vector.scalar_tensor_tensor(
                                out=tile[:, m, tap:SEQ], in0=PS[:, 4 * b.odd + 2 * m, 0:SEQ - tap], scalar=w,
                                in1=tile[:, m, tap:SEQ], op0=ALU.mult, op1=ALU.add)
                            if tap == 1:
                                ins.then_inc(sem(f"{name}_near"), 1)
                    retire(ins, s, b)
                    if k == 1:
                        dve.wait_ge(psum_free[1], i + (s.held[1] + 1))
                        dve.wait_ge(sem(f"{name}_silu"), i + 1)
                        vector.tensor_tensor(TC[:, :, 0:SEQ], TA[:, :, 0:SEQ], TB[:, :, 0:SEQ], ALU.mult
                                             ).then_inc(sem(f"{name}_prod"), 1)
                        hidden_rest(name, i, SEQ)

                walk(dve, split, s, FH, 2, body)

            def hidden_rest(name, i, tok):
                dve.wait_ge(sem(f"{name}_hi"), i + 1)
                vector.tensor_tensor(G_lo[:, bass.ds(i * 2, 2), 0:tok], TC[:, :, 0:tok],
                                     G_hi[:, bass.ds(i * 2, 2), 0:tok].bitcast(FP32), ALU.subtract
                                     ).then_inc(sem(f"{name}_lo"), 1)

            def up_second(name, tok):
                s = st[name]

                def body(i, step, k):
                    if k == 0:
                        return
                    b = At(k, step, i)
                    used(At(s.c + k, step, i))
                    dve.wait_ge(psum_free[0], i + (s.held[0] + 1))
                    for m in range(2):
                        ins = vector.tensor_tensor(halves(TC[:, m, 0:tok], tok), halves(TA[:, m, 0:tok], tok),
                                                   pview(b, m, tok), ALU.mult)
                    retire(ins, s, b)
                    hidden_rest(name, i, tok)

                walk(dve, split, s, FH, 2, body)

            def modulation(c0, c1, done):
                dve.wait_ge(sem("ada_used"), c1)
                vector.tensor_tensor(mod[:, c0:c1], PS[:, 7, c0:c1], vec("b_ada", c0, c1 - c0), ALU.add
                                     ).then_inc(sem(done + "_sum"), 1)
                dve.wait_ge(sem(done + "_sum"), 1)
                vector.tensor_scalar(mod1[:, c0:c1], mod[:, c0:c1], 1.0, None, ALU.add).then_inc(sem(done), 1)

            vector.memset(inv_v[:, :], 1.0 / P)
            vector.memset(one[:, :], 1.0)
            vector.memset(inv_d[:, :], 1.0 / D).then_inc(sem("consts"), 1)
            dve.wait_ge(sem("vec_loaded"), 16)
            split(At(0), words[0])
            modulation(0, ADA_FIRST, "mod_first")
            dve.wait_ge(sem("mod_first"), 1)
            norm(LN_IN)
            splits(st["fox"], 8)
            dve.wait_ge(sem("band_loaded"), 16)
            vector.tensor_copy(BAND0[:, :], BAND[:, :, 0]).then_inc(sem("band_far"), 1)
            dve.wait_ge(sem("band_far"), 1)
            vector.tensor_tensor(BAND[:, :, :], BAND[:, :, :],
                                 BAND0[:, :].rearrange("p (h o) -> p h o", o=1).to_broadcast([P, HEADS, 2 * P]),
                                 ALU.subtract).then_inc(sem("band_near"), 1)
            dve.wait_ge(sem("band_near"), 1)
            vector.memset(BAND[CHUNK:P, :, P + CHUNK:2 * P], NEG).then_inc(sem("band_bias"), 1)
            dve.wait_ge(psum_free[0], st["band"].held[0])
            vector.scalar_tensor_tensor(out=F[:, 1, :], in0=F[:, 0, :], scalar=-1.0, in1=F[:, 0, :], op0=ALU.mult,
                                        op1=ALU.max).then_inc(sem("fox_abs"), 1)
            vector.tensor_scalar(F[:, 0, :], F[:, 0, :], 0.0, None, ALU.min).then_inc(sem("fox_min"), 1)
            dve.wait_ge(sem("fox_log"), 1)
            dve.wait_ge(sem("fox_min"), 1)
            vector.tensor_tensor(F[:, 0, :], F[:, 0, :], F[:, 1, :], ALU.subtract).then_inc(sem("fox_logsig"), 1)
            dve.wait_ge(sem("fox_logsig"), 1)
            vector.tensor_tensor_scan(F[:, 2, :], one[0:HEADS, :].to_broadcast([HEADS, SEQ]), F[:, 0, :], 0.0,
                                      ALU.mult, ALU.subtract).then_inc(sem("fox_decay"), 1)
            attend(fox)
            splits(st["band"], 6)
            modulation(ADA_FIRST, ADA, "mod_rest")
            attend(band)
            dve.wait_ge(sem("mod_rest"), 1)
            merge("merge1", M_hi, M_lo)
            residual_sum("out1", 2, "g1", SEQ, META)
            norm(LN_1)
            norm(LN_MID)
            dve.wait_ge(sem("merge1_lo"), 5)
            up_first("up1")
            residual_sum("down1", 1, "g2", SEQ, META)
            norm(LN_2)
            norm(RMS_1)
            up_second("up2", TOK)
            residual_sum("down2", 1, 0.5, TOK, 0)
            norm(RMS_MIX)
            splits(st["win"], 4)
            dve.wait_ge(psum_free[0], st["gla"].held[0])
            vector.scalar_tensor_tensor(out=TB[:, :, :], in0=TA[:, :, :], scalar=-1.0, in1=TA[:, :, :], op0=ALU.mult,
                                        op1=ALU.max).then_inc(sem("z_abs"), 1)
            vector.tensor_scalar(TA[:, :, :], TA[:, :, :], 0.0, None, ALU.min).then_inc(sem("z_min"), 1)
            dve.wait_ge(sem("z_log"), 1)
            dve.wait_ge(sem("z_min"), 1)
            vector.tensor_tensor(TA[:, :, :], TA[:, :, :], TB[:, :, :], ALU.subtract).then_inc(sem("z_logsig"), 1)
            dve.wait_ge(sem("z_logsig"), 1)
            dve.wait_ge(sem("mix_const_loaded"), 48)
            for m in range(2):
                vector.tensor_tensor_scan(LE[:, m, :], RESET[:, :], TA[:, m, :], 0.0, ALU.mult, ALU.add
                                          ).then_inc(sem("b_sum"), 1)
            dve.wait_ge(sem("b_sum"), 2)
            for m in range(2):
                vector.tensor_tensor(LL[:, m, 0:META], LE[:, m, META - 1:META].to_broadcast([P, META]),
                                     LE[:, m, 0:META], ALU.subtract)
                b_of = LE[:, m, META:TOK].rearrange("p (n c) -> p n c", c=CHUNK)
                ins = vector.tensor_tensor(LL[:, m, META:TOK].rearrange("p (n c) -> p n c", c=CHUNK),
                                           b_of[:, :, CHUNK - 1:CHUNK].to_broadcast([P, GLA_CHUNKS, CHUNK]),
                                           b_of, ALU.subtract)
            ins.then_inc(sem("b_ready"), 1)
            attend(win)
            s = st["gla"]
            dve.wait_ge(sem("decays"), 1)
            for k in range(2):
                split(At(s.c + k + 1), words[s.c + k + 1])
                used(At(s.c + k))
                for m in range(2):
                    ps = pview(At(k), m, TOK)
                    if k == 0:
                        ins = vector.scalar_tensor_tensor(out=halves(LQ[:, m, :], TOK), in0=ps, scalar=HEAD ** -0.5,
                                                          in1=halves(LE[:, m, :], TOK), op0=ALU.mult, op1=ALU.mult)
                    else:
                        vector.tensor_tensor(halves(LK[:, m, :], TOK), halves(TB[:, m, :], TOK), ps, ALU.mult)
                        ins = vector.tensor_tensor(halves(LL[:, m, :], TOK), halves(LL[:, m, :], TOK), ps, ALU.mult)
                retire(ins, s, At(k))
            for k in range(2, 4):
                split(At(s.c + k + 1), words[s.c + k + 1])
            vector.memset(AM[:, :, :, :], 0.0).then_inc(sem("am_zero"), 1)
            dve.wait_ge(sem("kv_ready"), 1)
            for n in range(GLA_CHUNKS):
                for m in range(2):
                    kv = kv_at(m, n)
                    if n == 0:
                        ins = vector.tensor_copy(S[:, m, 0, :], kv)
                    else:
                        dve.wait_ge(sem("state_ready"), 2 * (n - 1) + m + 1)
                        t = META + n * CHUNK - 1
                        ins = vector.scalar_tensor_tensor(out=S[:, m, n, :], in0=S[:, m, n - 1, :], scalar=LE[:, m, t:t + 1],
                                                          in1=kv, op0=ALU.mult, op1=ALU.add)
                    ins.then_inc(sem("state_ready"), 1)
            dve.wait_ge(sem("am_zero"), 1)
            for h in range(GLA_HEADS):
                dve.wait_ge(sem("att_ready"), h + 1)
                vector.copy_predicated(AM[:, h, :, :],
                                       tri.bitcast(mybir.dt.uint32).rearrange("p (o c) -> p o c", o=1).to_broadcast([P, NB, P]),
                                       PS[:, h, :].rearrange("p (n c) -> p n c", c=P)).then_inc(sem("am_ready"), 1)
            dve.wait_ge(sem("og_sum"), 1)
            vector.tensor_scalar(small[:, 1, :], PS[:, 0, 0:GLA_HEADS * NB], RMS_EPS, None, ALU.add
                                 ).then_inc(sem("og_variance"), 1)
            dve.wait_ge(sem("og_deviation"), 1)
            vector.reciprocal(small[:, 3, :], small[:, 2, :]).then_inc(sem("og_inverse"), 1)
            dve.wait_ge(sem("og_spread"), 1)
            for h in range(GLA_HEADS):
                vector.scalar_tensor_tensor(out=OG[:, h, :], in0=OG[:, h, :], scalar=vec("gla_out_norm"),
                                            in1=PS[:, 4 + h, :], op0=ALU.mult, op1=ALU.mult
                                            ).then_inc(sem("og_normed"), 1)
            dve.wait_ge(sem("og_normed"), GLA_HEADS)
            for k in range(4, 6):
                split(At(s.c + k + 1), words[s.c + k + 1])
                dve.wait_ge(psum_free[k % 2], s.held[k % 2] + k // 2 + 1)
                if k == 5:
                    dve.wait_ge(sem("o2_lo"), 1)
                vector.tensor_tensor(TB[:, :, 0:SEQ], OG[:, 2 * k - 8:2 * k - 6, :], TA[:, :, 0:SEQ], ALU.mult
                                     ).then_inc(sem("og_gated"), 1)
                dve.wait_ge(sem("o2_hi"), k - 3)
                vector.tensor_tensor(O2_lo[:, 2 * k - 4:2 * k - 2, :], TB[:, :, 0:SEQ],
                                     O2_hi[:, 2 * k - 4:2 * k - 2, :].bitcast(FP32), ALU.subtract).then_inc(sem("o2_lo"), 1)
            dve.wait_ge(sem("o2_lo"), 2)
            merge("merge2", M_hi, M_lo)
            residual_sum("out2", 2, None, SEQ, META)
            norm(RMS_2)
            up_second("up3", SEQ)
            residual_sum("down3", 1, 0.5, SEQ, META)
            norm(RMS_OUT)


def kernel(**inputs):
    import ml_dtypes
    import numpy as np
    import concourse.bacc as bacc
    from concourse.bass_utils import run_bass_kernel_spmd

    a = {k: np.asarray(v) for k, v in inputs.items()}

    def chunked(w, width=2 * P):
        k, n = w.shape
        return w.reshape(k // P, P, n // width, width).transpose(2, 1, 0, 3).reshape(n // width, P, k // P * width)

    def down_chunks(w):
        return w.reshape(2, FH, P, KT, P).transpose(3, 0, 2, 1, 4).reshape(2 * KT, P, WD)

    def cols(v):
        return v.reshape(-1, P).T

    def features(x):
        return x.T.reshape(KT, P, -1).transpose(1, 0, 2)

    def merge_chunks(gate_one, gate_two, one, two):
        g1, g2, b = chunked(gate_one), chunked(gate_two), chunked(np.concatenate([one, two]))
        return [c[m] for m in range(4) for c in (g1, g2, b)]

    def up_chunks(first, second):
        f, s = chunked(first), chunked(second)
        return [c[m] for m in range(FH) for c in (f, s)]

    w1, w2 = a["w_in"][0], a["w_in_2"][0]
    fq, fk, fv, ff, bq, bk, bv, ga, gb = np.split(w1, np.cumsum([512, 512, 512, 8, 512, 512, 512, D]), axis=1)
    (aq, ak, av, gq, gk, gv, gr, low, ga2, gb2) = np.split(w2, np.cumsum([512, 128, 128, 256, 256, 512, 512, RANK, D]), axis=1)
    head_order = [h for t in range(4) for h in (t, 4 + t)]
    aq = aq.reshape(D, HEADS, HEAD)[:, head_order].reshape(D, 512)
    branch_att = a["w_branch_att_2"][0].reshape(HEADS, HEAD, D)[head_order].reshape(512, D)
    wts = []
    for v, q, k in ((fv, fq, fk), (bv, bq, bk)):
        wts += [*chunked(v), *chunked(q), *chunked(k)]
    wts += merge_chunks(ga, gb, a["w_br_fox"][0], a["w_br_chunk"][0])
    wts += [*chunked(a["w_out"][0])]
    wts += up_chunks(a["w_up"][0][:, :D_FF], a["w_up"][0][:, D_FF:])
    wts += up_chunks(a["ffn1_w_gate_2"][0], a["ffn1_w_up_2"][0])
    wts += [*chunked(aq), *chunked(np.concatenate([ak, av], axis=1))]
    wts += [*chunked(gq), *chunked(gk), *chunked(gv), *chunked(gr)]
    wts += merge_chunks(ga2, gb2, branch_att, a["w_branch_gla_2"][0])
    wts += [*chunked(a["w_out_2"][0])]
    wts += up_chunks(a["ffn2_w_gate_2"][0], a["ffn2_w_up_2"][0])
    f_at, low_at = 3 * 512, 512 + 256 + 512 + 1024
    forget = chunked(w1[:, f_at:f_at + P], P)[0].reshape(P, 2, WF).transpose(1, 0, 2)
    lowrank = chunked(w2[:, low_at:low_at + P], P)
    ident = np.eye(P, dtype=np.float32)
    key, query = np.arange(P)[:, None], np.arange(P)[None, :]
    within = (key <= query) & (key // CHUNK == query // CHUNK)
    cf = np.concatenate([ident, ident[::-1], within.astype(np.float32)], axis=1)
    causal = np.where(np.arange(P)[None, :] <= np.arange(P)[:, None], 0.0, NEG)
    cb = np.concatenate([ident, causal], axis=1).astype(ml_dtypes.bfloat16)
    qpos, kpos = np.arange(P)[:, None] + P, np.arange(2 * P)[None, :]
    reach = (kpos // CHUNK <= qpos // CHUNK) & (kpos // CHUNK >= qpos // CHUNK - 2)
    distance = np.where(reach, -np.abs(qpos - kpos).astype(np.float32), NEG)
    slopes = [2.0 ** -(h + 1) * ident for h in range(HEADS)]
    cw = np.concatenate([distance, *slopes], axis=1).astype(ml_dtypes.bfloat16)
    reset = np.ones((P, TOK), np.float32)
    reset[:, [0, *range(META, TOK, CHUNK)]] = 0.0
    f32 = np.float32
    parts = {
        "c": cols(a["c"][0]), "b_ada": cols(a["b_ada"][0]), "conv_w": cols(a["conv_w"][0]), "conv_b": cols(a["conv_b"][0]),
        "ln1_g": cols(a["ln1_g"][0]), "ln1_b": cols(a["ln1_b"][0]), "ln2_g": cols(a["ln2_g"][0]),
        "ln2_b": cols(a["ln2_b"][0]), "ffn1_norm": cols(a["ffn1_norm_2"][0]), "mix_norm": cols(a["mix_norm_2"][0]),
        "ffn2_norm": cols(a["ffn2_norm_2"][0]), "final_norm": cols(a["final_norm_2"]),
        "gla_gate_b": cols(a["gla_gate_b_2"][0]), "gla_out_norm": cols(a["gla_out_norm_2"][0]),
        "sinks": np.broadcast_to(a["att_sinks_2"][0], (P, HEADS)),
        "b_f": np.concatenate([a["b_f"][0], np.zeros(P - HEADS, f32)])[:, None],
    }
    rel = a["rel_bias"][0][:, 1:][:, ::-1]
    band_rel = np.concatenate([np.repeat(rel[:, :1], P - 1, axis=1), rel, rel[:, -1:]], axis=1)
    arrays = {
        "wts": np.stack(wts), "wfg": forget, "wlow": lowrank,
        "wdown": np.concatenate([down_chunks(a["w_down"][0]), down_chunks(a["ffn1_w_down_2"][0]),
                                 down_chunks(a["ffn2_w_down_2"][0])]),
        "wada": chunked(a["w_ada"][0], P), "vecs": np.concatenate([parts[n] for n, _ in VECS], axis=1),
        "xT": features(a["x"][0]), "metaT": features(a["meta_tokens_2"]), "gate_w": a["gla_gate_w_2"][0],
        "band_rel": band_rel, "cf": cf, "cb": cb, "cw": cw, "cs": reset,
    }
    arrays = {k: np.ascontiguousarray(v) for k, v in arrays.items()}
    nc = bacc.Bacc("TRN2", target_bir_lowering=False, num_devices=1)
    aps = {k: nc.dram_tensor(f"in_{k}", v.shape, mybir.dt.from_np(v.dtype), kind="ExternalInput").ap()
           for k, v in arrays.items()}
    out = nc.dram_tensor("out", (P, KT, SEQ), FP32, kind="ExternalOutput").ap()
    build_program(nc, **aps, out=out)
    r = run_bass_kernel_spmd(nc, [{f"in_{k}": v for k, v in arrays.items()}], core_ids=[0])
    y = r.results[0]["out"]
    return np.ascontiguousarray(y.transpose(2, 1, 0).reshape(1, SEQ, D))
```

```python
from contextlib import ExitStack

import concourse.bass as bass
from concourse import mybir

FP32 = mybir.dt.float32
F32R = mybir.dt.float32r
BF16 = mybir.dt.bfloat16
ACT = mybir.ActivationFunctionType
ALU = mybir.AluOpType
AX = mybir.AxisListType

P = 128
D = 1024
KT = D // P
SEQ = 512
META = 16
TOK = SEQ + META
HALF = TOK // 2
NB = SEQ // P
HEAD = 64
HEADS = 8
CHUNK = 64
D_FF = 2816
FT = D_FF // P
FH = FT // 2
GLA_HEADS = 4
GLA_CHUNKS = SEQ // CHUNK
RANK = 16
SCORE_BANK = (0, 1, 6)
ADA = 6 * KT
ADA_AHEAD = 11
ADA_GROUPS = ((0, 3), (3, 6), (6, 9), (9, 11))
ADA_FIRST = 2 * KT
ADA_STEP = 3
ALPHA = 2.0 ** 0.25
LN_EPS = 1e-5
RMS_EPS = 1e-6
NEG = -1e30
WC = KT * 2 * P
WF = KT // 2 * P
WG = KT * P
WD = FH * P
QSCALE = HEAD ** -0.5

VECS = [("b_ada", ADA), ("conv_w", 3 * 2 * FT), ("conv_b", 2 * FT), ("ln1_g", KT), ("ln1_b", KT),
        ("ln2_g", KT), ("ln2_b", KT), ("ffn1_norm", KT), ("mix_norm", KT), ("ffn2_norm", KT),
        ("final_norm", KT), ("gla_gate_b", 2), ("gla_out_norm", 1), ("sinks", HEADS), ("b_f", 1)]
VEC_AT = {name: sum(w for _, w in VECS[:i]) for i, (name, _) in enumerate(VECS)}
VEC_COLS = sum(w for _, w in VECS)

STAGES = [("fox", [WC] * 6 + [WF] * 2, 7), ("band", [WC] * 6, 6), ("merge1", [WC] * 12, 12),
          ("out1", [WC] * 4, 4), ("up1", [WC] * FT, FT), ("down1", [WD] * 2 * KT, KT),
          ("up2", [WC] * FT, FT), ("down2", [WD] * 2 * KT, KT), ("win", [WC] * 3 + [WG], 5),
          ("gla", [WC] * 6, 6), ("merge2", [WC] * 12, 12), ("out2", [WC] * 4, 4),
          ("up3", [WC] * FT, FT), ("down3", [WD] * 2 * KT, KT)]


class Stage:

    def __init__(self, chunk, array_index, words, held, n_batches):
        self.c, self.at, self.words, self.held, self.n = chunk, array_index, words, held, n_batches


def plan():
    stages, c, held, seen = {}, 0, [0, 0], {}
    for name, words, nb in STAGES:
        stages[name] = Stage(c, seen.get(words[0], 0), words, tuple(held), nb)
        for w in words:
            seen[w] = seen.get(w, 0) + 1
        c += len(words)
        held[0] += (nb + 1) // 2
        held[1] += nb // 2
    return stages, [w for _, ws, _ in STAGES for w in ws]


class At:

    def __init__(self, base, step=0, i=0):
        self.base, self.step, self.i = base, step, i

    def __add__(self, k):
        return At(self.base + k, self.step, self.i)

    @property
    def n(self):
        return self.step * self.i + self.base if self.step else self.base

    @property
    def half(self):
        return (self.step // 2) * self.i + self.base // 2 if self.step else self.base // 2

    @property
    def odd(self):
        return self.base % 2


def build_program(nc, wts, wfg, wlow, wdown, wada, cond, vecs, xT, metaT, gate_w, band_rel, cf, cb, cw, cs, out):
    st, words = plan()
    n_chunks = len(words)
    with ExitStack() as ctx:
        def sb(name, shape, dt, scope=ctx):
            return scope.enter_context(nc.sbuf_tensor(name, shape, dt))

        sems = {}

        def sem(name):
            if name not in sems:
                sems[name] = ctx.enter_context(nc.semaphore(name))
            return sems[name]

        W_raw = sb("W_raw", [P, 2, WC], FP32)
        W_hi = sb("W_hi", [P, 2, WC], F32R)
        W_lo = sb("W_lo", [P, 2, WC], F32R)
        X = sb("X", [P, KT, TOK], FP32)
        H_hi = sb("H_hi", [P, KT, TOK], F32R)
        with ExitStack() as over:
            SQ = sb("SQ", [P, KT, TOK], FP32, over)
        H_lo = sb("H_lo", [P, KT, TOK], F32R)
        T = sb("T", [P, 3 * 2 * TOK], FP32)
        V = sb("V", [P, VEC_COLS], FP32)
        CF = sb("CF", [P, 3 * P], FP32)
        CB = sb("CB", [P, 2 * P], BF16)
        mod = sb("mod", [P, ADA], FP32)
        mod1 = sb("mod1", [P, ADA], FP32)
        inv_d = sb("inv_d", [P, P], FP32)
        eps_ln = sb("eps_ln", [P, 1], FP32)
        eps_rms = sb("eps_rms", [P, 1], FP32)
        inv_v = sb("inv_v", [P, 1], FP32)
        one = sb("one", [P, 1], FP32)
        small = sb("small", [P, 3, GLA_HEADS * NB], FP32)
        stat = sb("stat", [P, 6, HEADS * NB], FP32)
        A_ring = T[:, 0:3 * D].rearrange("p (s w) -> p s w", s=3)
        TA, TB, TC = (T[:, n * 2 * TOK:(n + 1) * 2 * TOK].rearrange("p (m t) -> p m t", m=2) for n in range(3))
        GW = TC[0:RANK, 1, 0:2 * P]
        ident, exch, tri = CF[:, 0:P], CF[:, P:2 * P], CF[:, 2 * P:3 * P]
        ident_b, causal_b = CB[:, 0:P], CB[:, P:2 * P]
        with ExitStack() as over:
            G_hi = sb("G_hi", [P, FT, TOK], F32R, over)
            G_lo = sb("G_lo", [P, FT, TOK], F32R, over)
        with ExitStack() as over:
            N1 = sb("N1", [P, KT, TOK], FP32, over)
            N2 = sb("N2", [P, KT, TOK], FP32, over)
            DEV = sb("DEV", [P, TOK], FP32, over)
            INV = sb("INV", [P, TOK], FP32, over)
            A_ahead = sb("A_ahead", [P, ADA_AHEAD, D], FP32, over)
        with ExitStack() as over:
            Q = sb("Q", [P, 4, SEQ], FP32, over)
            K = sb("K", [P, 4, SEQ], FP32, over)
            VT = sb("VT", [P, NB, SEQ], FP32, over)
            PR = sb("PR", [P, 3, SEQ], FP32, over)
            PT = sb("PT", [P, 3, SEQ], FP32, over)
            O_hi = sb("O_hi", [P, 8, SEQ], F32R, over)
            O_lo = sb("O_lo", [P, 8, SEQ], F32R, over)
            BAND = sb("BAND", [P, HEADS, 2 * P], FP32, over)
            BAND0 = sb("BAND0", [P, HEADS], FP32, over)
            F = sb("F", [HEADS, 3, SEQ], FP32, over)
            silu_c = sb("silu_c", [P, D], FP32, over)
        with ExitStack() as over:
            M_hi = sb("M_hi", [P, KT, SEQ], F32R, over)
            M_lo = sb("M_lo", [P, KT, SEQ], F32R, over)
        late = 4 * (5 * 2 * P + 2 * GLA_CHUNKS * P + GLA_HEADS * NB * P + GLA_HEADS * SEQ)
        early = 4 * (4 * SEQ + TOK + (NB + 1) * P + 6 * 3 * P)
        with ExitStack() as over:
            WQ = sb("WQ", [P, 4, SEQ], FP32, over)
            WK = sb("WK", [P, TOK], FP32, over)
            WV = sb("WV", [P, NB + 1, P], FP32, over)
            WPR = sb("WPR", [P, 3, 3 * P], FP32, over)
            WPT = sb("WPT", [P, 3, 3 * P], FP32, over)
            sb("filler", [P, (late - early) // 4], FP32, over)
            LQ = sb("LQ", [P, 2, TOK], FP32, over)
            LK = sb("LK", [P, 2, TOK], FP32, over)
            O2_hi = sb("O2_hi", [P, 8, SEQ], F32R, over)
            O2_lo = sb("O2_lo", [P, 8, SEQ], F32R, over)
            LE = sb("LE", [P, 2, TOK], FP32, over)
            LL = sb("LL", [P, 2, TOK], FP32, over)
            LV = sb("LV", [P, NB + 1, SEQ], FP32, over)
            RESET = sb("RESET", [P, TOK], FP32, over)
            CW = sb("CW", [P, 2 * P + HEADS * P], BF16, over)
        with ExitStack() as over:
            KL = sb("KL", [P, NB + 1, 2 * P], FP32, over)
            S = sb("S", [P, 2, GLA_CHUNKS, P], FP32, over)
            AM = sb("AM", [P, GLA_HEADS, NB, P], FP32, over)
            OG = sb("OG", [P, GLA_HEADS, SEQ], FP32, over)
        PS = ctx.enter_context(nc.psum_tensor("PS", [P, 8, 512], FP32))

        w_loaded = [sem("w_loaded0"), sem("w_loaded1")]
        w_hi, w_lo = sem("w_hi"), sem("w_lo")
        w_used = sem("w_used")
        psum_free = [sem("psum_free0"), sem("psum_free1")]

        def vec(name, k=0, n=1):
            return V[:, bass.ds(k + VEC_AT[name], n)]

        def free_at(s, b):
            return psum_free[b.odd], b.half + s.held[b.odd]

        def pview(b, m, tok):
            bank = 4 * b.odd + 2 * m
            return PS[:, bank:bank + 1, :] if tok == SEQ else PS[:, bank:bank + 2, 0:HALF]

        def halves(tile, tok):
            return tile.rearrange("p (a t) -> p a t", a=1 if tok == SEQ else 2)

        def spans(tok):
            return [(0, SEQ)] if tok == SEQ else [(0, HALF), (HALF, HALF)]


        class Attention:

            def __init__(self, before, heads, width, blocks, probs, turned, o_hi, o_lo, out_at, sinks):
                self.before, self.width, self.blocks, self.sinks = before, width, blocks, sinks
                self.probs, self.turned, self.o_hi, self.o_lo, self.out_at = probs, turned, o_hi, o_lo, out_at
                self.items = [(h, n // 2, n % 2, i) for n, h in enumerate(heads) for i in range(NB)]
                self.n = len(self.items)

            def sem(self, what):
                return sem(f"att_{what}")

            def reach(self, what, value):
                if what in ("key_max", "sink", "total"):
                    return self.sem(what), value
                return self.sem(what), value + self.before * (HEADS // 2 if what in ("out_hi", "out_lo") else HEADS * NB)

        def first_blocks(i):
            return [(P * j, P, j) for j in range(i + 1)]

        def window_blocks(i):
            meta = [(0, META, NB)]
            return meta + ([(META, P, i)] if i == 0 else [(META, P, i - 1), (META + P, P, i)])

        fox = Attention(0, range(HEADS), lambda i: P * (i + 1), first_blocks, PR, PT, O_hi, O_lo, 0, False)
        band = Attention(1, range(HEADS), lambda i: P * (i + 1), first_blocks, PR, PT, O_hi, O_lo, 4, False)
        win = Attention(2, [h for t in range(4) for h in (t, 4 + t)],
                        lambda i: META + P * (1 if i == 0 else 2), window_blocks, WPR, WPT, O2_hi, O2_lo, 0, True)

        class Norm:

            def __init__(self, number, at, tok, center, gain, bias, to, src_ready):
                self.number, self.at, self.tok, self.center = number, at, tok, center
                self.gain, self.bias, self.to, self.src_ready = gain, bias, to, src_ready

            def sem(self, what):
                return sem(f"norm_{what}")

            def count(self, what):
                if what in ("mean", "centred") and not self.center:
                    return 0
                if (what == "scaled" and self.to == "N") or (what == "rounded" and self.to != "H"):
                    return 0
                return KT if what in ("centred", "squared", "scaled", "rounded", "done") else 1

            def reach(self, what, value):
                return self.sem(what), value + sum(m.count(what) for m in norms[:self.number])

            def src(self, k):
                return X[:, k, self.at:self.at + self.tok]

            def centred(self, k):
                return N1[:, k, 0:self.tok] if self.center else self.src(k)

            def spread(self, bank):
                return PS[:, bank:bank + 1, :] if self.tok == SEQ else PS[:, bank:bank + 2, 0:HALF]

            def outs(self, bank):
                return [(PS[:, bank + n, 0:tn], (t0, tn)) for n, (t0, tn) in enumerate(spans(self.tok))]

        MODCOL = {"sh1": 0, "sc1": KT, "g1": 2 * KT, "sh2": 3 * KT, "sc2": 4 * KT, "g2": 5 * KT}

        def modv(name):
            return lambda k: mod[:, MODCOL[name] + k:MODCOL[name] + k + 1]

        def modv1(name):
            return lambda k: mod1[:, MODCOL[name] + k:MODCOL[name] + k + 1]

        def vv(name):
            return lambda k: vec(name, k)

        norms = [
            Norm(0, META, SEQ, True, modv1("sc1"), modv("sh1"), "H", None),
            Norm(1, META, SEQ, True, vv("ln1_g"), vv("ln1_b"), "X", "out1_x"),
            Norm(2, META, SEQ, True, modv1("sc2"), modv("sh2"), "H", 1),
            Norm(3, META, SEQ, True, vv("ln2_g"), vv("ln2_b"), "X", "down1_x"),
            Norm(4, 0, TOK, False, vv("ffn1_norm"), None, "H", 3),
            Norm(5, 0, TOK, False, vv("mix_norm"), None, "H", "down2_x"),
            Norm(6, META, SEQ, False, vv("ffn2_norm"), None, "H", "out2_x"),
            Norm(7, META, SEQ, False, vv("final_norm"), None, "N", "down3_x"),
        ]
        LN_IN, LN_1, LN_MID, LN_2, RMS_1, RMS_MIX, RMS_2, RMS_OUT = norms

        def wait_src(eng, n, k):
            if n.src_ready is None:
                eng.wait_ge(sem("x_loaded"), 16)
            elif isinstance(n.src_ready, int):
                eng.wait_ge(*norms[n.src_ready].reach("done", k + 1))
            else:
                eng.wait_ge(sem(n.src_ready), k + 1)

        def kv_at(m, n):
            if n == 0:
                return PS[:, 3, m * P:(m + 1) * P]
            return PS[:, 4 + 2 * m + (n - 1) % 2, (n - 1) // 2 * P:((n - 1) // 2 + 1) * P]

        def squares(h):
            return T[:, h * SEQ:(h + 1) * SEQ]

        def retire(ins, s, b):
            return ins.then_inc(psum_free[b.odd], 1)

        def walk(eng, split, s, n, per, body):
            end = s.c + n * per
            after = words[end] if end < n_chunks else 0

            def chunks_of_round(i, step, size_after):
                for k in range(per):
                    nxt = At(s.c + k + 1, step, i)
                    size = s.words[0] if k < per - 1 else size_after
                    if size:
                        split(nxt, size)
                    body(i, step, k)

            if after == s.words[0]:
                with eng.Fori(0, n) as i:
                    chunks_of_round(i, per, after)
            else:
                with eng.Fori(0, n - 1) as i:
                    chunks_of_round(i, per, s.words[0])
                chunks_of_round(n - 1, per, after)

        block = ctx.enter_context(nc.Block())

        @block.sync
        def _(sp):
            def load(src, c):
                if not (c.step == 0 and c.base < 2):
                    sp.wait_ge(w_lo, (c + -1).n)
                n = src.shape[-1]
                sp.dma_start(W_raw[:, c.odd, 0:n], src).then_inc(w_loaded[c.odd], 16)

            def pick(arr, n):
                return arr[bass.ds(n, 1)].rearrange("o p n -> (o p) n")

            def load_stage(name):
                s = st[name]
                arr = wdown if s.words[0] == WD else wts
                special = {"fox": wfg, "win": wlow}.get(name)
                plain = [w for w in s.words if w == s.words[0]]
                if name in ("fox", "win", "band", "gla") or s.c < 2:
                    for k in range(len(plain)):
                        load(pick(arr, s.at + k), At(s.c + k))
                else:
                    with sp.Fori(0, len(plain) // 2) as i:
                        for k in range(2):
                            load(pick(arr, 2 * i + (s.at + k)), At(s.c + k, 2, i))
                if special is not None:
                    for k in range(len(s.words) - len(plain)):
                        load(pick(special, k), At(s.c + len(plain) + k))

            sp.dma_start(X[:, :, META:TOK], xT).then_inc(sem("x_loaded"), 16)
            for g, (t0, t1) in enumerate(ADA_GROUPS):
                sp.dma_start(A_ahead[:, t0:t1, :], wada[t0:t1].rearrange("s p n -> p s n")).then_inc(sem(f"ada_ahead{g}"), 16)
            for name, _, _ in STAGES:
                load_stage(name)
            for k in range(KT):
                sp.wait_ge(*RMS_OUT.reach("done", k + 1))
                sp.dma_start(out[:, k, :], N2[:, k, 0:SEQ]).then_inc(sem("stored"), 16)
            sp.wait_ge(sem("stored"), 16 * KT)

        @block.gpsimd
        def _(pool):
            def small_load(dst, src, name):
                pool.dma_start(dst, src).then_inc(sem(name), 16)

            small_load(silu_c[:, :], cond, "cond_loaded")
            small_load(V[:, :], vecs, "vec_loaded")
            small_load(CF[:, :], cf, "const_loaded")
            small_load(CB[:, :], cb, "const_loaded")
            small_load(X[:, :, 0:META], metaT, "meta_loaded")
            for t in range(ADA_AHEAD, ADA):
                if t >= ADA_AHEAD + 3:
                    pool.wait_ge(sem("ada_used"), t - 2)
                small_load(A_ring[:, (t - ADA_AHEAD) % 3, :], wada[t], f"ada_loaded{(t - ADA_AHEAD) % 3}")
                if t == ADA_FIRST:
                    rows = bass.AP(tensor=band_rel.tensor, offset=0, ap=[[1, P], [3 * P, HEADS], [1, 2 * P]])
                    small_load(BAND[:, :, :], rows, "band_loaded")
            pool.wait_ge(*RMS_MIX.reach("scaled", 1))
            small_load(RESET[:, :], cs, "mix_const_loaded")
            small_load(CW[:, :], cw, "mix_const_loaded")
            small_load(GW[:, :], gate_w, "mix_const_loaded")
            pool.wait_ge(sem("mix_const_loaded"), 48)

        @block.tensor
        def _(pe):
            def mm(*a, **kw):
                return nc.tensor.matmul(*a, **kw)

            def chunk_ready(c):
                pe.wait_ge(w_lo, (c + 1).n)

            def group_free(s, b):
                sm, v = free_at(s, b)
                if not (isinstance(v, int) and v == 0):
                    pe.wait_ge(sm, v)

            def tile_ready(ready, k):
                if ready is not None:
                    pe.wait_ge(*ready(k))

            def normed(n):
                return lambda k: n.reach("done", k + 1)

            def merged(name):
                return lambda k: (sem(f"{name}_lo"), k // 2 + 2)

            def feature_tile(outs, slot, off, stride, ks, act_hi, act_lo, start=True, stop=True, ready=None):
                for n, k in enumerate(ks):
                    tile_ready(ready, k)
                    a = off + n * stride
                    wh, wl = W_hi[:, slot, a:a + P], W_lo[:, slot, a:a + P]
                    for m, (w, x) in enumerate(((wh, act_hi), (wh, act_lo), (wl, act_hi))):
                        for o, (t0, tn) in outs:
                            last = mm(o, w, x[:, k, t0:t0 + tn], start=start and n == 0 and m == 0,
                                      stop=stop and n == len(ks) - 1 and m == 2)
                return last

            def token_tile(o, tok0, slot, off, stride, n_cols, ready=None):
                for k in range(KT):
                    tile_ready(ready, k)
                    a = off + k * stride
                    wh, wl = W_hi[:, slot, a:a + n_cols], W_lo[:, slot, a:a + n_cols]
                    xh, xl = H_hi[:, k, tok0:tok0 + P], H_lo[:, k, tok0:tok0 + P]
                    for m, (x, w) in enumerate(((xh, wh), (xh, wl), (xl, wh))):
                        last = mm(o, x, w, start=k == 0 and m == 0, stop=k == KT - 1 and m == 2)
                return last

            def outs_of(b, m, tok, at):
                v = pview(b, m, tok)
                return [(v[:, n, 0:tn], (at + t0, tn)) for n, (t0, tn) in enumerate(spans(tok))]

            def project(s, c, b, tok, at, act_hi=H_hi, act_lo=H_lo, tiles=2, ready=None):
                chunk_ready(c)
                group_free(s, b)
                for m in range(tiles):
                    last = feature_tile(outs_of(b, m, tok, at), c.odd, m * P, tiles * P, range(KT), act_hi, act_lo,
                                        ready=ready if m == 0 else None)
                last.then_inc(w_used, 1)

            def statistic(n, bank, tile_of, ready, done):
                for k in range(KT):
                    ready(k)
                    for o, (t0, tn) in n.outs(bank):
                        last = mm(o, inv_d[:, :], tile_of(k)[:, t0:t0 + tn], start=k == 0, stop=k == KT - 1)
                last.then_inc(done, 1)

            def norm(n, after):
                for g in range(2):
                    if after[g]:
                        pe.wait_ge(psum_free[g], after[g])
                if n.center:
                    statistic(n, 4, n.src, lambda k: wait_src(pe, n, k), n.sem("mean"))
                statistic(n, 6, lambda k: SQ[:, k, 0:n.tok], lambda k: pe.wait_ge(*n.reach("squared", k + 1)), n.sem("variance"))

            def attend(a, scores):
                for t in range(a.n + 3):
                    if t < a.n:
                        h, pair, half, i = a.items[t]
                        if t >= 3:
                            pe.wait_ge(*a.reach("prob", t - 2))
                        scores(PS[:, SCORE_BANK[t % 3], :], h, pair, half, i).then_inc(a.sem("scores"), 1)
                    if 2 <= t <= a.n + 1:
                        u = t - 2
                        i = a.items[u][3]
                        pe.wait_ge(*a.reach("normed", u + 1))
                        if u >= 2:
                            pe.wait_ge(*a.reach("copied", u - 1))
                        for n, (col, keys, _) in enumerate(a.blocks(i)):
                            last = nc.tensor.transpose(PS[0:keys, 2 + u % 2, n * P:(n + 1) * P],
                                                       a.probs[:, u % 3, col:col + keys], ident)
                        last.then_inc(a.sem("turned"), 1)
                    if t >= 3:
                        v = t - 3
                        h, pair, half, i = a.items[v]
                        pe.wait_ge(*a.reach("copied", v + 1))
                        if v % (2 * NB) == 0 and pair >= 2:
                            pe.wait_ge(*a.reach("out_lo", pair - 1))
                        o = PS[HEAD * half:HEAD * half + HEAD, 4 + pair % 2, i * P:(i + 1) * P]
                        blocks = a.blocks(i)
                        for n, (_, keys, tile) in enumerate(blocks):
                            values = (WV[0:keys, tile, HEAD * half:HEAD * half + HEAD] if a is win
                                      else VT[0:keys, tile, HEAD * h:HEAD * h + HEAD])
                            last = mm(o, values, a.turned[0:keys, v % 3, n * P:(n + 1) * P],
                                      start=n == 0, stop=n == len(blocks) - 1)
                        last.then_inc(a.sem("pv"), 1)
                pe.wait_ge(*a.reach("prob", a.n))
                pe.wait_ge(*a.reach("copied", a.n))
                pe.wait_ge(*a.reach("out_lo", a.n // (2 * NB)))

            def rows_of(half):
                return slice(HEAD * half, HEAD * half + HEAD)

            def fox_scores(o, h, pair, half, i):
                w = P * (i + 1)
                r = rows_of(half)
                mm(o[:, 0:w], Q[r, pair, i * P:(i + 1) * P], K[r, pair, 0:w], start=True, stop=False)
                mm(o[:, 0:w], ident[0:HEADS, h:h + 1].to_broadcast([HEADS, P]), F[:, 2, 0:w], start=False, stop=True)
                return mm(o[:, i * P:w], ident_b, causal_b, start=False, stop=True, skip_group_check=True)

            def band_scores(o, h, pair, half, i):
                w = P * (i + 1)
                r = rows_of(half)
                mm(o[:, 0:w], Q[r, pair, i * P:(i + 1) * P], K[r, pair, 0:w], start=True, stop=True)
                bias = BAND[:, h, P:2 * P] if i == 0 else BAND[:, h, :]
                return mm(o[:, max(i - 1, 0) * P:w], exch, bias, start=False, stop=True, skip_group_check=True)

            def window_scores(o, h, pair, half, i):
                w = win.width(i)
                r = rows_of(half)
                q = WQ[r, pair, i * P:(i + 1) * P]
                first_key = META + max(i - 1, 0) * P
                distance = CW[:, P:2 * P] if i == 0 else CW[:, 0:2 * P]
                mm(o[:, META:w], q, WK[r, first_key:first_key + w - META], start=True, stop=False)
                mm(o[:, META:w], CW[:, (2 + h) * P:(3 + h) * P], distance, start=False, stop=True)
                return mm(o[:, 0:META], q, WK[r, 0:META], start=False, stop=True, skip_group_check=True)

            def values_fox(s, k, ready=None):
                c, b = At(s.c + k), At(k)
                chunk_ready(c)
                group_free(s, b)
                for blk in range(NB):
                    last = token_tile(PS[:, 4 * b.odd + blk // 2, blk % 2 * 256:blk % 2 * 256 + 256],
                                      META + blk * P, c.odd, 0, 2 * P, 2 * P, ready if blk == 0 else None)
                last.then_inc(w_used, 1)

            def merge(name, o_hi, o_lo):
                s = st[name]
                with pe.Fori(0, 2) as i:
                    for mp in range(2):
                        for part in range(2):
                            k = 3 * mp + part
                            project(s, At(s.c + k, 6, i), At(k, 6, i), SEQ, META)
                        k = 3 * mp + 2
                        c, b = At(s.c + k, 6, i), At(k, 6, i)
                        chunk_ready(c)
                        group_free(s, b)
                        for m in range(2):
                            for br in range(2):
                                o = PS[:, 4 * b.odd + 2 * m + br, :]
                                last = feature_tile([(o, (0, SEQ))], c.odd, br * 4 * 2 * P + m * P, 2 * P,
                                                    range(4 * br, 4 * br + 4), o_hi, o_lo)
                        last.then_inc(w_used, 1)

            def project_all(name, n, tok, at, act_hi=H_hi, act_lo=H_lo, ready=None):
                s = st[name]
                if ready is not None:
                    for k in range(2):
                        project(s, At(s.c + k), At(k), tok, at, act_hi, act_lo, ready=ready if k == 0 else None)
                with pe.Fori(0 if ready is None else 1, n) as i:
                    for k in range(2):
                        project(s, At(s.c + k, 2, i), At(k, 2, i), tok, at, act_hi, act_lo)

            def down(name, tok, split):
                s = st[name]
                with pe.Fori(0, KT // 2) as i:
                    for b2 in range(2):
                        b = At(b2, 2, i)
                        for half in range(2):
                            c = At(s.c + 2 * b2 + half, 4, i)
                            chunk_ready(c)
                            if half == 0:
                                group_free(s, b)
                            pe.wait_ge(split, (FH - 1) // 2 + 1 if half == 0 else FH)
                            ks = range(FH * half, FH * half + FH)
                            feature_tile(outs_of(b, 0, tok, 0), c.odd, 0, P, ks, G_hi, G_lo,
                                         start=half == 0, stop=half == 1).then_inc(w_used, 1)

            pe.wait_ge(sem("consts"), 1)
            norm(LN_IN, (0, 0))
            s = st["fox"]
            for k in range(2):
                values_fox(s, k, normed(LN_IN) if k == 0 else None)
            for k in range(2, 6):
                project(s, At(s.c + k), At(k), SEQ, META)
            for half in range(2):
                c, b = At(s.c + 6 + half), At(6)
                chunk_ready(c)
                if half == 0:
                    group_free(s, b)
                feature_tile(outs_of(b, 0, SEQ, META), c.odd, 0, P, range(4 * half, 4 * half + 4), H_hi, H_lo,
                             start=half == 0, stop=half == 1).then_inc(w_used, 1)
            pe.wait_ge(psum_free[0], st["band"].held[0])
            pe.wait_ge(psum_free[1], st["band"].held[1])
            pe.wait_ge(sem("fox_decay"), 1)
            pe.wait_ge(sem("const_loaded"), 32)
            attend(fox, fox_scores)
            s = st["band"]
            for k in range(2):
                values_fox(s, k)
            for k in range(2, 6):
                project(s, At(s.c + k), At(k), SEQ, META)
            pe.wait_ge(psum_free[0], st["merge1"].held[0])
            pe.wait_ge(psum_free[1], st["merge1"].held[1])
            pe.wait_ge(sem("band_bias"), 1)
            attend(band, band_scores)
            merge("merge1", O_hi, O_lo)
            project_all("out1", 2, SEQ, 0, M_hi, M_lo, ready=merged("merge1"))
            norm(LN_1, st["up1"].held)
            norm(LN_MID, st["up1"].held)
            project_all("up1", FH, SEQ, META, ready=normed(LN_MID))
            down("down1", SEQ, sem("up1_lo"))
            norm(LN_2, st["up2"].held)
            norm(RMS_1, st["up2"].held)
            project_all("up2", FH, TOK, 0, ready=normed(RMS_1))
            down("down2", TOK, sem("up2_lo"))
            norm(RMS_MIX, st["win"].held)
            s = st["win"]
            for k in range(2):
                project(s, At(s.c + k), At(k), SEQ, META, ready=normed(RMS_MIX) if k == 0 else None)
            c, b = At(s.c + 2), At(2)
            chunk_ready(c)
            group_free(s, b)
            feature_tile(outs_of(b, 0, TOK, 0), c.odd, 0, 2 * P, range(KT), H_hi, H_lo)
            for blk in range(NB):
                token_tile(PS[:, 4 * b.odd + 2, blk * P:(blk + 1) * P], META + blk * P, c.odd, P, 2 * P, P)
            token_tile(PS[:, 4 * b.odd + 3, 0:P], 0, c.odd, P, 2 * P, P).then_inc(w_used, 1)
            project(s, At(s.c + 3), At(3), TOK, 0, tiles=1)
            b = At(4)
            group_free(s, b)
            pe.wait_ge(psum_free[1], s.held[1] + 2)
            pe.wait_ge(sem("mix_const_loaded"), 48)
            for m in range(2):
                for o, (t0, tn) in outs_of(b, m, TOK, 0):
                    last = mm(o, GW[:, m * P:(m + 1) * P], TC[0:RANK, 0, t0:t0 + tn], start=True, stop=True)
            last.then_inc(sem("z_ready"), 1)
            pe.wait_ge(psum_free[0], st["gla"].held[0])
            pe.wait_ge(psum_free[1], st["gla"].held[1])
            attend(win, window_scores)
            s = st["gla"]
            for k in range(2):
                project(s, At(s.c + k), At(k), TOK, 0)
            for k in range(2, 4):
                c, b = At(s.c + k), At(k)
                chunk_ready(c)
                group_free(s, b)
                for blk in range(NB):
                    token_tile(PS[:, 4 * b.odd + blk // 2, blk % 2 * 256:blk % 2 * 256 + 256],
                               META + blk * P, c.odd, 0, 2 * P, 2 * P)
                token_tile(PS[:, 4 * b.odd + 2, 0:256], 0, c.odd, 0, 2 * P, 2 * P).then_inc(w_used, 1)
            pe.wait_ge(psum_free[0], s.held[0] + 2)
            pe.wait_ge(psum_free[1], s.held[1] + 2)
            for n in range(NB + 1):
                t0 = META + n * P if n < NB else 0
                for m in range(2):
                    last = nc.tensor.transpose(PS[:, n // 2, n % 2 * 256 + m * P:n % 2 * 256 + (m + 1) * P],
                                               LL[:, m, t0:t0 + P], ident)
            last.then_inc(sem("kl_turned"), 1)
            pe.wait_ge(sem("kl_ready"), 1)
            for m in range(2):
                for n in range(GLA_CHUNKS):
                    blk, r = (NB, slice(0, META)) if n == 0 else ((n - 1) // 2, rows_of((n - 1) % 2))
                    for hh in range(2):
                        h = 2 * m + hh
                        last = mm(kv_at(m, n)[rows_of(hh), :],
                                  KL[r, blk, h * HEAD:(h + 1) * HEAD], LV[r, blk, h * P:(h + 1) * P],
                                  start=True, stop=True)
            last.then_inc(sem("kv_ready"), 1)
            for h in range(GLA_HEADS):
                if h == GLA_HEADS - 1:
                    pe.wait_ge(sem("state_ready"), 2)
                for n in range(NB):
                    t0 = META + n * P
                    r = rows_of(h % 2)
                    last = mm(PS[:, h, n * P:(n + 1) * P], LK[r, h // 2, t0:t0 + P], LQ[r, h // 2, t0:t0 + P],
                              start=True, stop=True)
                last.then_inc(sem("att_ready"), 1)
            pe.wait_ge(sem("state_ready"), 2 * GLA_CHUNKS)
            for h in range(GLA_HEADS):
                pe.wait_ge(sem("am_ready"), h + 1)
                for n in range(NB):
                    mm(PS[:, 4 + h, n * P:(n + 1) * P], LV[:, n, h * P:(h + 1) * P], AM[:, h, n, :], start=True, stop=True)
                    for c in (2 * n, 2 * n + 1):
                        r, t0 = rows_of(h % 2), META + c * CHUNK
                        last = mm(PS[:, 4 + h, c * CHUNK:(c + 1) * CHUNK], S[r, h // 2, c, :],
                                  LQ[r, h // 2, t0:t0 + CHUNK], start=False, stop=True, skip_group_check=True)
                last.then_inc(sem("og_raw"), 1)
            for h in range(GLA_HEADS):
                pe.wait_ge(sem("og_squared"), h + 1)
                for n in range(NB):
                    last = mm(PS[:, 0, h * NB + n:h * NB + n + 1], squares(h)[:, n * P:(n + 1) * P], inv_v[:, 0:1],
                              start=True, stop=True)
            last.then_inc(sem("og_sum"), 1)
            pe.wait_ge(sem("og_variance"), 1)
            project(s, At(s.c + 4), At(4), SEQ, META)
            pe.wait_ge(sem("og_inverse"), 1)
            for h in range(GLA_HEADS):
                for n in range(NB):
                    last = mm(PS[:, 4 + h, n * P:(n + 1) * P],
                              small[:, 2, h * NB + n:h * NB + n + 1].to_broadcast([P, P]), ident, start=True, stop=True)
            last.then_inc(sem("og_spread"), 1)
            pe.wait_ge(sem("og_normed"), GLA_HEADS)
            project(s, At(s.c + 5), At(5), SEQ, META)
            pe.wait_ge(sem("o2_lo"), 2)
            merge("merge2", O2_hi, O2_lo)
            project_all("out2", 2, SEQ, 0, M_hi, M_lo, ready=merged("merge2"))
            norm(RMS_2, st["up3"].held)
            project_all("up3", FH, SEQ, META, ready=normed(RMS_2))
            down("down3", SEQ, sem("up3_lo"))
            norm(RMS_OUT, [st["down3"].held[g] + KT // 2 for g in range(2)])
        @block.scalar
        def _(act):
            def activate(*a, **kw):
                return nc.scalar.activation(*a, **kw)

            def split(c, size):
                act.wait_ge(w_loaded[c.odd], (c.half + 1) * 16)
                if not (c.step == 0 and c.base < 2):
                    act.wait_ge(w_used, (c + -1).n)
                activate(W_hi[:, c.odd, 0:size], W_raw[:, c.odd, 0:size], ACT.Copy).then_inc(w_hi, 1)

            def used(c):
                act.wait_ge(w_used, (c + 1).n)

            def norm(n, between=lambda: None):
                if n.center:
                    for k in range(KT):
                        act.wait_ge(*n.reach("centred", k + 1))
                        activate(SQ[:, k, 0:n.tok], n.centred(k), ACT.Square).then_inc(n.sem("squared"), 1)
                else:
                    for k in range(KT):
                        wait_src(act, n, k)
                        if n is RMS_1 and k == 0:
                            act.wait_ge(sem("meta_loaded"), 16)
                        activate(SQ[:, k, 0:n.tok], n.src(k), ACT.Square).then_inc(n.sem("squared"), 1)
                act.wait_ge(*n.reach("variance", 1))
                activate(halves(DEV[:, 0:n.tok], n.tok), n.spread(6), ACT.Sqrt, bias=(eps_ln if n.center else eps_rms)[:, :]
                         ).then_inc(n.sem("deviation"), 1)
                between()
                if n.to == "N":
                    return
                for k in range(KT):
                    act.wait_ge(*n.reach("scaled", k + 1))
                    dst = H_hi[:, k, n.at:n.at + n.tok] if n.to == "H" else n.src(k)
                    if n.bias is None:
                        ins = activate(dst, N2[:, k, 0:n.tok], ACT.Copy)
                    else:
                        ins = activate(dst, N2[:, k, 0:n.tok], ACT.Identity, bias=n.bias(k))
                    ins.then_inc(n.sem("rounded" if n.to == "H" else "done"), 1)

            def attend(a):
                def put_out(pair):
                    act.wait_ge(*a.reach("pv", 2 * NB * (pair + 1)))
                    activate(a.o_hi[:, a.out_at + pair, :], PS[:, 4 + pair % 2, :], ACT.Copy).then_inc(a.sem("out_hi"), 1)

                for t in range(a.n + 2):
                    if t < a.n:
                        h, pair, half, i = a.items[t]
                        act.wait_ge(*a.reach("max", t + 1))
                        if t >= 3:
                            act.wait_ge(*a.reach("turned", t - 2))
                        w = a.width(i)
                        activate(a.probs[:, t % 3, 0:w], PS[:, SCORE_BANK[t % 3], 0:w], ACT.Exp, bias=stat[:, 0, t:t + 1],
                                 accum_out=stat[:, 1, t:t + 1]).then_inc(a.sem("prob"), 1)
                        if a.sinks:
                            activate(stat[:, 4, t:t + 1], vec("sinks", h), ACT.Exp,
                                     bias=stat[:, 0, t:t + 1]).then_inc(a.sem("sink"), 1)
                    if t >= 2:
                        u = t - 2
                        act.wait_ge(*a.reach("turned", u + 1))
                        if u >= 3:
                            act.wait_ge(*a.reach("pv", u - 2))
                        n = 0
                        for n, (_, keys, _) in enumerate(a.blocks(a.items[u][3])):
                            if keys < P:
                                activate(a.turned[0:keys, u % 3, n * P:(n + 1) * P],
                                         PS[0:keys, 2 + u % 2, n * P:(n + 1) * P], ACT.Copy)
                        n0 = 1 if a.blocks(0)[0][1] < P else 0
                        activate(a.turned[:, u % 3, n0 * P:(n + 1) * P], PS[:, 2 + u % 2, n0 * P:(n + 1) * P],
                                 ACT.Copy).then_inc(a.sem("copied"), 1)
                        if t % (2 * NB) == 4 and t > 2 * NB:
                            put_out(t // (2 * NB) - 1)
                put_out(a.n // (2 * NB) - 1)

            def copies(s, k, plan_of):
                split(At(s.c + k + 1), words[s.c + k + 1])
                used(At(s.c + k))
                for dst, src, scale in plan_of[:-1]:
                    activate(dst, src, ACT.Copy, scale=scale)
                dst, src, scale = plan_of[-1]
                retire(activate(dst, src, ACT.Copy, scale=scale), s, At(k))

            def value_plan(k, dst, meta=False):
                g = 4 * (k % 2)
                col = 256 * (k % 2)
                p = [(dst[:, 2 * bb:2 * bb + 2, col:col + 256], PS[:, g + bb, :].rearrange("p (b n) -> p b n", b=2), 1.0)
                     for bb in range(2)]
                if meta:
                    p.append((dst[0:META, NB, col:col + 256], PS[0:META, g + 2, 0:256], 1.0))
                return p

            def tile_plan(k, dst, first, scale):
                g = 4 * (k % 2)
                return [(dst[:, first + m, :], PS[:, g + 2 * m, :], scale) for m in range(2)]

            def merge(name, m_hi):
                s = st[name]

                def body(i, step, k):
                    mp, part = k // 3, k % 3
                    c, b = At(s.c + k, step, i), At(k, step, i)
                    rnd = mp + 2 * i
                    if part < 2:
                        used(c)
                        if part == 0:
                            act.wait_ge(sem(f"{name}_lo"), rnd + 1)
                        dst = (TA, TB)[part]
                        for m in range(2):
                            ins = activate(dst[:, m, 0:SEQ], PS[:, 4 * b.odd + 2 * m, :], ACT.Sigmoid)
                        retire(ins, s, b)
                    else:
                        act.wait_ge(sem(f"{name}_sum"), rnd + 1)
                        activate(m_hi[:, bass.ds(2 * rnd, 2), :], TC[:, :, 0:SEQ], ACT.Copy).then_inc(sem(f"{name}_hi"), 1)

                walk(act, split, s, 2, 6, body)

            def up_first(name):
                s = st[name]

                def body(i, step, k):
                    c, b = At(s.c + k, step, i), At(k, step, i)
                    if k == 1:
                        act.wait_ge(psum_free[0], i + (s.held[0] + 1))
                        activate(TA[:, :, 0:SEQ], TA[:, :, 0:SEQ], ACT.Silu).then_inc(sem(f"{name}_silu"), 1)
                    used(c)
                    if k == 0:
                        act.wait_ge(sem(f"{name}_prod"), i + 1)
                    for m in range(2):
                        col = i * 2 + (k * FT + m)
                        activate((TA, TB)[k][:, m, 0:SEQ], PS[:, 4 * b.odd + 2 * m, :], ACT.Identity,
                                 bias=vec("conv_b", col), scale=vec("conv_w", col + 2 * 2 * FT)
                                 ).then_inc(sem(f"{name}_tap"), 1)
                    if k == 1:
                        act.wait_ge(sem(f"{name}_prod"), i + 2)
                        activate(G_hi[:, bass.ds(i * 2, 2), 0:SEQ], TC[:, :, 0:SEQ], ACT.Copy).then_inc(sem(f"{name}_hi"), 1)

                walk(act, split, s, FH, 2, body)

            def up_second(name, tok):
                s = st[name]

                def body(i, step, k):
                    c, b = At(s.c + k, step, i), At(k, step, i)
                    if k == 0:
                        used(c)
                        act.wait_ge(psum_free[1], i + s.held[1])
                        for m in range(2):
                            ins = activate(halves(TA[:, m, 0:tok], tok), pview(b, m, tok), ACT.Silu)
                        retire(ins, s, b)
                    else:
                        act.wait_ge(psum_free[1], i + (s.held[1] + 1))
                        activate(G_hi[:, bass.ds(i * 2, 2), 0:tok], TC[:, :, 0:tok], ACT.Copy).then_inc(sem(f"{name}_hi"), 1)

                walk(act, split, s, FH, 2, body)

            def scale_residual(name, n, per):
                s = st[name]

                def body(i, step, k):
                    if k == 0:
                        activate(X[:, bass.ds(i * (KT // n), KT // n), META:TOK], X[:, bass.ds(i * (KT // n), KT // n), META:TOK],
                                 ACT.Copy, scale=ALPHA).then_inc(sem(f"{name}_alpha"), 1)

                walk(act, split, s, n, per, body)

            def only_split(name, n, per):
                walk(act, split, st[name], n, per, lambda i, step, k: None)

            act.wait_ge(sem("cond_loaded"), 16)
            activate(silu_c[:, :], silu_c[:, :], ACT.Silu).then_inc(sem("silu_c"), 1)
            act.wait_ge(sem("vec_loaded"), 16)
            norm(LN_IN, lambda: split(At(0), words[0]))
            s = st["fox"]
            for k in range(2):
                copies(s, k, value_plan(k, VT))
            for k in range(2, 4):
                copies(s, k, tile_plan(k, Q, 2 * (k - 2), QSCALE))
            for k in range(4, 6):
                copies(s, k, tile_plan(k, K, 2 * (k - 4), 1.0))
            split(At(s.c + 7), words[s.c + 7])
            split(At(s.c + 8), words[s.c + 8])
            used(At(s.c + 7))
            retire(activate(F[:, 0, :], PS[0:HEADS, 0, :], ACT.Identity, bias=V[0:HEADS, VEC_AT["b_f"]:VEC_AT["b_f"] + 1]),
                   s, At(6))
            act.wait_ge(sem("fox_abs"), 1)
            activate(F[:, 1, :], F[:, 1, :], ACT.Exp, scale=-1.0).then_inc(sem("fox_exp"), 1)
            act.wait_ge(sem("fox_exp"), 1)
            activate(F[:, 1, :], F[:, 1, :], ACT.Ln, bias=one[0:HEADS, :]).then_inc(sem("fox_log"), 1)
            attend(fox)
            s = st["band"]
            for k in range(2):
                copies(s, k, value_plan(k, VT))
            for k in range(2, 4):
                copies(s, k, tile_plan(k, Q, 2 * (k - 2), QSCALE))
            for k in range(4, 6):
                copies(s, k, tile_plan(k, K, 2 * (k - 4), 1.0))
            attend(band)
            act.wait_ge(sem("ada_used"), ADA)
            merge("merge1", M_hi)
            scale_residual("out1", 2, 2)
            norm(LN_1)
            norm(LN_MID)
            up_first("up1")
            scale_residual("down1", 4, 4)
            norm(LN_2)
            norm(RMS_1)
            up_second("up2", TOK)
            only_split("down2", 4, 4)
            norm(RMS_MIX)
            s = st["win"]
            for k in range(2):
                copies(s, k, tile_plan(k, WQ, 2 * k, QSCALE))
            copies(s, 2, [(halves(WK[:, :], TOK), PS[:, 0:2, 0:HALF], 1.0),
                          (WV[:, 0:NB, :], PS[:, 2, :].rearrange("p (b n) -> p b n", b=NB), 1.0),
                          (WV[0:META, NB, :], PS[0:META, 3, 0:P], 1.0)])
            k = 3
            split(At(s.c + k + 1), words[s.c + k + 1])
            used(At(s.c + k))
            retire(activate(halves(TC[0:RANK, 0, :], TOK), PS[0:RANK, 4:6, 0:HALF], ACT.Copy), s, At(3))
            act.wait_ge(sem("z_ready"), 1)
            for m in range(2):
                ins = activate(halves(TA[:, m, :], TOK), PS[:, 2 * m:2 * m + 2, 0:HALF], ACT.Identity,
                               bias=vec("gla_gate_b", m))
            retire(ins, s, At(4))
            attend(win)
            s = st["gla"]
            split(At(s.c + 1), words[s.c + 1])
            act.wait_ge(sem("z_abs"), 1)
            activate(TB[:, :, :], TB[:, :, :], ACT.Exp, scale=-1.0).then_inc(sem("z_exp"), 1)
            act.wait_ge(sem("z_exp"), 1)
            activate(TB[:, :, :], TB[:, :, :], ACT.Ln, bias=one[:, :]).then_inc(sem("z_log"), 1)
            act.wait_ge(sem("b_ready"), 1)
            activate(TB[:, :, :], LE[:, :, :], ACT.Exp, scale=-1.0 / 16.0)
            activate(LL[:, :, :], LL[:, :, :], ACT.Exp, scale=1.0 / 16.0)
            activate(LE[:, :, :], LE[:, :, :], ACT.Exp, scale=1.0 / 16.0).then_inc(sem("decays"), 1)
            split(At(s.c + 2), words[s.c + 2])
            for k in range(2, 4):
                copies(s, k, value_plan(k, LV, meta=True))
            act.wait_ge(sem("kl_turned"), 1)
            for n in range(0, NB + 1, 2):
                w = 2 if n < NB else 1
                ins = activate(KL[:, n:n + w, :], PS[:, n // 2, 0:w * 256].rearrange("p (b n) -> p b n", b=w), ACT.Copy)
            ins.then_inc(sem("kl_ready"), 1)
            for h in range(GLA_HEADS):
                act.wait_ge(sem("og_raw"), h + 1)
                activate(OG[:, h, :], PS[:, 4 + h, :], ACT.Copy)
                activate(squares(h), PS[:, 4 + h, :], ACT.Square).then_inc(sem("og_squared"), 1)
            act.wait_ge(sem("og_variance"), 1)
            activate(small[:, 1, :], small[:, 0, :], ACT.Sqrt).then_inc(sem("og_deviation"), 1)
            for k in range(4, 6):
                split(At(s.c + k + 1), words[s.c + k + 1])
                used(At(s.c + k))
                if k == 5:
                    act.wait_ge(sem("og_gated"), 1)
                for m in range(2):
                    ins = activate(TA[:, m, 0:SEQ], PS[:, 4 * (k % 2) + 2 * m, :], ACT.Silu)
                retire(ins, s, At(k))
                act.wait_ge(sem("og_gated"), k - 3)
                activate(O2_hi[:, 2 * k - 4:2 * k - 2, :], TB[:, :, 0:SEQ], ACT.Copy).then_inc(sem("o2_hi"), 1)
            merge("merge2", M_hi)
            only_split("out2", 2, 2)
            norm(RMS_2)
            up_second("up3", SEQ)
            only_split("down3", 4, 4)
            norm(RMS_OUT)

        @block.vector
        def _(dve):
            vector = nc.vector

            def split(c, size):
                dve.wait_ge(w_hi, (c + 1).n)
                vector.tensor_tensor(W_lo[:, c.odd, 0:size], W_raw[:, c.odd, 0:size],
                                     W_hi[:, c.odd, 0:size].bitcast(FP32), ALU.subtract).then_inc(w_lo, 1)

            def used(c):
                dve.wait_ge(w_used, (c + 1).n)

            def norm(n, between=lambda: None, before_scale=lambda: None):
                if n.center:
                    dve.wait_ge(*n.reach("mean", 1))
                    for k in range(KT):
                        vector.tensor_tensor(halves(n.centred(k), n.tok), halves(n.src(k), n.tok), n.spread(4),
                                             ALU.subtract).then_inc(n.sem("centred"), 1)
                between()
                dve.wait_ge(*n.reach("deviation", 1))
                vector.reciprocal(INV[:, 0:n.tok], DEV[:, 0:n.tok]).then_inc(n.sem("inverse"), 1)
                before_scale()
                dve.wait_ge(*n.reach("inverse", 1))

                def leave(k):
                    dve.wait_ge(*n.reach("rounded", k + 1))
                    hi = H_hi[:, k, n.at:n.at + n.tok].bitcast(FP32)
                    lo = H_lo[:, k, n.at:n.at + n.tok]
                    if n.bias is None:
                        ins = vector.tensor_tensor(lo, N2[:, k, 0:n.tok], hi, ALU.subtract)
                    else:
                        ins = vector.scalar_tensor_tensor(out=lo, in0=N2[:, k, 0:n.tok], scalar=n.bias(k), in1=hi,
                                                          op0=ALU.add, op1=ALU.subtract)
                    ins.then_inc(n.sem("done"), 1)

                for k in range(KT):
                    vector.scalar_tensor_tensor(out=N2[:, k, 0:n.tok], in0=n.centred(k), scalar=n.gain(k),
                                                in1=INV[:, 0:n.tok], op0=ALU.mult, op1=ALU.mult
                                                ).then_inc(n.sem("done" if n.to == "N" else "scaled"), 1)
                    if n.to == "H" and k:
                        leave(k - 1)
                if n.to == "H":
                    leave(KT - 1)

            def attend(a):
                def put_out(pair):
                    dve.wait_ge(*a.reach("out_hi", pair + 1))
                    at = a.out_at + pair
                    vector.tensor_tensor(a.o_lo[:, at, :], PS[:, 4 + pair % 2, :], a.o_hi[:, at, :].bitcast(FP32),
                                         ALU.subtract).then_inc(a.sem("out_lo"), 1)

                for t in range(a.n + 1):
                    if t < a.n:
                        h, pair, half, i = a.items[t]
                        dve.wait_ge(*a.reach("scores", t + 1))
                        w = a.width(i)
                        if a.sinks:
                            vector.tensor_reduce(stat[:, 3, t:t + 1], PS[:, SCORE_BANK[t % 3], 0:w], AX.X, ALU.max
                                                 ).then_inc(a.sem("key_max"), 1)
                            dve.wait_ge(*a.reach("key_max", t + 1))
                            vector.tensor_scalar(stat[:, 0, t:t + 1], stat[:, 3, t:t + 1], vec("sinks", h), -1.0,
                                                 ALU.max, ALU.mult).then_inc(a.sem("max"), 1)
                        else:
                            vector.tensor_reduce(stat[:, 0, t:t + 1], PS[:, SCORE_BANK[t % 3], 0:w], AX.X, ALU.max, negate=True
                                                 ).then_inc(a.sem("max"), 1)
                    if t >= 1:
                        u = t - 1
                        w = a.width(a.items[u][3])
                        total = stat[:, 1, u:u + 1]
                        if a.sinks:
                            dve.wait_ge(*a.reach("sink", u + 1))
                            total = stat[:, 5, u:u + 1]
                            vector.tensor_tensor(total, stat[:, 1, u:u + 1], stat[:, 4, u:u + 1], ALU.add
                                                 ).then_inc(a.sem("total"), 1)
                            dve.wait_ge(*a.reach("total", u + 1))
                        dve.wait_ge(*a.reach("prob", u + 1))
                        vector.reciprocal(stat[:, 2, u:u + 1], total).then_inc(a.sem("inverse"), 1)
                        dve.wait_ge(*a.reach("inverse", u + 1))
                        vector.tensor_scalar(a.probs[:, u % 3, 0:w], a.probs[:, u % 3, 0:w], stat[:, 2, u:u + 1], None,
                                             ALU.mult).then_inc(a.sem("normed"), 1)
                        if t % (2 * NB) == 5 and t > 2 * NB:
                            put_out(t // (2 * NB) - 1)
                put_out(a.n // (2 * NB) - 1)

            def splits(s, n, ada=ADA, ada_steps=KT):
                for k in range(n):
                    split(At(s.c + k + 1), words[s.c + k + 1])
                    if k < ada_steps:
                        take_ada(ada + k * ADA_STEP, ada + (k + 1) * ADA_STEP)

            def merge(name, m_hi, m_lo):
                s = st[name]
                dve.sem_inc(sem(f"{name}_lo"), 1)

                def body(i, step, k):
                    mp, part = k // 3, k % 3
                    if part < 2:
                        return
                    c, b = At(s.c + k, step, i), At(k, step, i)
                    rnd = mp + 2 * i
                    used(c)
                    dve.wait_ge(psum_free[1 - b.odd], (At(k - 1, step, i).half + s.held[1 - b.odd]) + 1)
                    for m in range(2):
                        for br in range(2):
                            tile = (TA, TB)[br][:, m, 0:SEQ]
                            ins = vector.tensor_tensor(tile, tile, PS[:, 4 * b.odd + 2 * m + br, :], ALU.mult)
                            if m == 1 and br == 1:
                                retire(ins, s, b)
                    dve.wait_ge(psum_free[b.odd], (b.half + s.held[b.odd]) + 1)
                    vector.tensor_tensor(TC[:, :, 0:SEQ], TA[:, :, 0:SEQ], TB[:, :, 0:SEQ], ALU.add
                                         ).then_inc(sem(f"{name}_sum"), 1)
                    dve.wait_ge(sem(f"{name}_hi"), rnd + 1)
                    vector.tensor_tensor(m_lo[:, bass.ds(2 * rnd, 2), :], TC[:, :, 0:SEQ],
                                         m_hi[:, bass.ds(2 * rnd, 2), :].bitcast(FP32), ALU.subtract
                                         ).then_inc(sem(f"{name}_lo"), 1)

                walk(dve, split, s, 2, 6, body)

            def residual_sum(name, tiles_per_batch, gain, tok, at):
                s = st[name]
                n, per = (2, 2) if tiles_per_batch == 2 else (4, 4)

                def body(i, step, k):
                    if tiles_per_batch == 1 and k % 2 == 0:
                        return
                    b = At(k if tiles_per_batch == 2 else k // 2, 2, i)
                    used(At(s.c + k, step, i))
                    if gain is not None and gain != 0.5 and (k == 0 or (tiles_per_batch == 1 and k == 1)):
                        dve.wait_ge(sem(f"{name}_alpha"), i + 1)
                    for m in range(tiles_per_batch):
                        f = (i * (n_tiles_per_round)) + (m + tiles_per_batch * b.base)
                        x = X[:, bass.ds(f, 1), at:at + tok].rearrange("p o t -> p (o t)")
                        ps = pview(b, m, tok)
                        if gain is None:
                            ins = vector.tensor_tensor(halves(x, tok), ps, halves(x, tok), ALU.add)
                        else:
                            g = 0.5 if gain == 0.5 else mod1[:, bass.ds(f + MODCOL[gain], 1)]
                            ins = vector.scalar_tensor_tensor(out=halves(x, tok), in0=ps, scalar=g, in1=halves(x, tok),
                                                              op0=ALU.mult, op1=ALU.add)
                        ins.then_inc(sem(f"{name}_x"), 1)
                    dve.wait_ge(sem(f"{name}_x"), (i * n_tiles_per_round) + tiles_per_batch * (b.base + 1))
                    dve.sem_inc(psum_free[b.odd], 1)

                n_tiles_per_round = 2 * tiles_per_batch
                walk(dve, split, s, n, per, body)

            def up_first(name):
                s = st[name]
                dve.sem_inc(sem(f"{name}_prod"), 1)

                def body(i, step, k):
                    b = At(k, step, i)
                    tile = (TA, TB)[k]
                    for tap in (1, 2):
                        for m in range(2):
                            if tap == 1:
                                dve.wait_ge(sem(f"{name}_tap"), i * 4 + (2 * k + m + 1))
                            else:
                                dve.wait_ge(sem(f"{name}_near"), i * 4 + (2 * k + m + 1))
                            w = vec("conv_w", i * 2 + (k * FT + m + (2 - tap) * 2 * FT))
                            ins = vector.scalar_tensor_tensor(
                                out=tile[:, m, tap:SEQ], in0=PS[:, 4 * b.odd + 2 * m, 0:SEQ - tap], scalar=w,
                                in1=tile[:, m, tap:SEQ], op0=ALU.mult, op1=ALU.add)
                            if tap == 1:
                                ins.then_inc(sem(f"{name}_near"), 1)
                    retire(ins, s, b)
                    if k == 1:
                        dve.wait_ge(psum_free[1], i + (s.held[1] + 1))
                        dve.wait_ge(sem(f"{name}_silu"), i + 1)
                        vector.tensor_tensor(TC[:, :, 0:SEQ], TA[:, :, 0:SEQ], TB[:, :, 0:SEQ], ALU.mult
                                             ).then_inc(sem(f"{name}_prod"), 1)
                        hidden_rest(name, i, SEQ)

                walk(dve, split, s, FH, 2, body)

            def hidden_rest(name, i, tok):
                dve.wait_ge(sem(f"{name}_hi"), i + 1)
                vector.tensor_tensor(G_lo[:, bass.ds(i * 2, 2), 0:tok], TC[:, :, 0:tok],
                                     G_hi[:, bass.ds(i * 2, 2), 0:tok].bitcast(FP32), ALU.subtract
                                     ).then_inc(sem(f"{name}_lo"), 1)

            def up_second(name, tok):
                s = st[name]

                def body(i, step, k):
                    if k == 0:
                        return
                    b = At(k, step, i)
                    used(At(s.c + k, step, i))
                    dve.wait_ge(psum_free[0], i + (s.held[0] + 1))
                    for m in range(2):
                        ins = vector.tensor_tensor(halves(TC[:, m, 0:tok], tok), halves(TA[:, m, 0:tok], tok),
                                                   pview(b, m, tok), ALU.mult)
                    retire(ins, s, b)
                    hidden_rest(name, i, tok)

                walk(dve, split, s, FH, 2, body)

            def take_ada(t0, t1):
                for t in range(t0, min(t1, ADA)):
                    if t < ADA_AHEAD:
                        for g, (first, _) in enumerate(ADA_GROUPS):
                            if t == first:
                                dve.wait_ge(sem(f"ada_ahead{g}"), 16)
                        w = A_ahead[:, t, :]
                    else:
                        slot, turn = (t - ADA_AHEAD) % 3, (t - ADA_AHEAD) // 3
                        dve.wait_ge(sem(f"ada_loaded{slot}"), 16 * (turn + 1))
                        w = A_ring[:, slot, :]
                    vector.scalar_tensor_tensor(out=w, in0=w, scalar=1.0, in1=silu_c[:, :], op0=ALU.mult, op1=ALU.mult,
                                                accum_out=mod[:, t:t + 1]).then_inc(sem("ada_used"), 1)

            def modulation(c0, c1, done):
                dve.wait_ge(sem("ada_used"), c1)
                vector.tensor_tensor(mod[:, c0:c1], mod[:, c0:c1], vec("b_ada", c0, c1 - c0), ALU.add
                                     ).then_inc(sem(done + "_sum"), 1)
                dve.wait_ge(sem(done + "_sum"), 1)
                vector.tensor_scalar(mod1[:, c0:c1], mod[:, c0:c1], 1.0, None, ALU.add).then_inc(sem(done), 1)

            vector.memset(inv_v[:, :], 1.0 / P)
            vector.memset(one[:, :], 1.0)
            vector.memset(eps_ln[:, :], LN_EPS)
            vector.memset(eps_rms[:, :], RMS_EPS)
            vector.memset(inv_d[:, :], 1.0 / D).then_inc(sem("consts"), 1)
            def first_modulation():
                dve.wait_ge(sem("silu_c"), 1)
                take_ada(0, 8)

            def last_modulation():
                take_ada(8, ADA_FIRST)
                dve.wait_ge(sem("vec_loaded"), 16)
                modulation(0, ADA_FIRST, "mod_first")
                split(At(0), words[0])
                dve.wait_ge(sem("mod_first"), 1)

            norm(LN_IN, first_modulation, last_modulation)
            splits(st["fox"], 8, ADA_FIRST, 6)
            dve.wait_ge(psum_free[0], st["band"].held[0])
            vector.scalar_tensor_tensor(out=F[:, 1, :], in0=F[:, 0, :], scalar=-1.0, in1=F[:, 0, :], op0=ALU.mult,
                                        op1=ALU.max).then_inc(sem("fox_abs"), 1)
            vector.tensor_scalar(F[:, 0, :], F[:, 0, :], 0.0, None, ALU.min).then_inc(sem("fox_min"), 1)
            dve.wait_ge(sem("fox_log"), 1)
            dve.wait_ge(sem("fox_min"), 1)
            vector.tensor_tensor(F[:, 0, :], F[:, 0, :], F[:, 1, :], ALU.subtract).then_inc(sem("fox_logsig"), 1)
            dve.wait_ge(sem("fox_logsig"), 1)
            vector.tensor_tensor_scan(F[:, 2, :], one[0:HEADS, :].to_broadcast([HEADS, SEQ]), F[:, 0, :], 0.0,
                                      ALU.mult, ALU.subtract).then_inc(sem("fox_decay"), 1)
            attend(fox)
            dve.wait_ge(sem("band_loaded"), 16)
            vector.tensor_copy(BAND0[:, :], BAND[:, :, 0]).then_inc(sem("band_far"), 1)
            dve.wait_ge(sem("band_far"), 1)
            vector.tensor_tensor(BAND[:, :, :], BAND[:, :, :],
                                 BAND0[:, :].rearrange("p (h o) -> p h o", o=1).to_broadcast([P, HEADS, 2 * P]),
                                 ALU.subtract).then_inc(sem("band_near"), 1)
            dve.wait_ge(sem("band_near"), 1)
            vector.memset(BAND[CHUNK:P, :, P + CHUNK:2 * P], NEG).then_inc(sem("band_bias"), 1)
            splits(st["band"], 6, ADA_FIRST + 6 * ADA_STEP)
            modulation(ADA_FIRST, ADA, "mod_rest")
            attend(band)
            dve.wait_ge(sem("mod_rest"), 1)
            merge("merge1", M_hi, M_lo)
            residual_sum("out1", 2, "g1", SEQ, META)
            norm(LN_1)
            norm(LN_MID)
            dve.wait_ge(sem("merge1_lo"), 5)
            up_first("up1")
            residual_sum("down1", 1, "g2", SEQ, META)
            norm(LN_2)
            norm(RMS_1)
            up_second("up2", TOK)
            residual_sum("down2", 1, 0.5, TOK, 0)
            norm(RMS_MIX)
            splits(st["win"], 4)
            attend(win)
            s = st["gla"]
            split(At(s.c + 1), words[s.c + 1])
            dve.wait_ge(psum_free[0], s.held[0])
            vector.scalar_tensor_tensor(out=TB[:, :, :], in0=TA[:, :, :], scalar=-1.0, in1=TA[:, :, :], op0=ALU.mult,
                                        op1=ALU.max).then_inc(sem("z_abs"), 1)
            vector.tensor_scalar(TA[:, :, :], TA[:, :, :], 0.0, None, ALU.min).then_inc(sem("z_min"), 1)
            dve.wait_ge(sem("z_log"), 1)
            dve.wait_ge(sem("z_min"), 1)
            vector.tensor_tensor(TA[:, :, :], TA[:, :, :], TB[:, :, :], ALU.subtract).then_inc(sem("z_logsig"), 1)
            dve.wait_ge(sem("z_logsig"), 1)
            dve.wait_ge(sem("mix_const_loaded"), 48)
            for m in range(2):
                vector.tensor_tensor_scan(LE[:, m, :], RESET[:, :], TA[:, m, :], 0.0, ALU.mult, ALU.add
                                          ).then_inc(sem("b_sum"), 1)
            dve.wait_ge(sem("b_sum"), 2)
            for m in range(2):
                vector.tensor_tensor(LL[:, m, 0:META], LE[:, m, META - 1:META].to_broadcast([P, META]),
                                     LE[:, m, 0:META], ALU.subtract)
                b_of = LE[:, m, META:TOK].rearrange("p (n c) -> p n c", c=CHUNK)
                ins = vector.tensor_tensor(LL[:, m, META:TOK].rearrange("p (n c) -> p n c", c=CHUNK),
                                           b_of[:, :, CHUNK - 1:CHUNK].to_broadcast([P, GLA_CHUNKS, CHUNK]),
                                           b_of, ALU.subtract)
            ins.then_inc(sem("b_ready"), 1)
            dve.wait_ge(sem("decays"), 1)
            for k in range(2):
                if k == 1:
                    split(At(s.c + 2), words[s.c + 2])
                used(At(s.c + k))
                for m in range(2):
                    ps = pview(At(k), m, TOK)
                    if k == 0:
                        ins = vector.scalar_tensor_tensor(out=halves(LQ[:, m, :], TOK), in0=ps, scalar=HEAD ** -0.5,
                                                          in1=halves(LE[:, m, :], TOK), op0=ALU.mult, op1=ALU.mult)
                    else:
                        vector.tensor_tensor(halves(LK[:, m, :], TOK), halves(TB[:, m, :], TOK), ps, ALU.mult)
                        ins = vector.tensor_tensor(halves(LL[:, m, :], TOK), halves(LL[:, m, :], TOK), ps, ALU.mult)
                retire(ins, s, At(k))
            for k in range(2, 4):
                split(At(s.c + k + 1), words[s.c + k + 1])
            vector.memset(AM[:, :, :, :], 0.0).then_inc(sem("am_zero"), 1)
            dve.wait_ge(sem("kv_ready"), 1)
            for n in range(GLA_CHUNKS):
                for m in range(2):
                    kv = kv_at(m, n)
                    if n == 0:
                        ins = vector.tensor_copy(S[:, m, 0, :], kv)
                    else:
                        dve.wait_ge(sem("state_ready"), 2 * (n - 1) + m + 1)
                        t = META + n * CHUNK - 1
                        ins = vector.scalar_tensor_tensor(out=S[:, m, n, :], in0=S[:, m, n - 1, :], scalar=LE[:, m, t:t + 1],
                                                          in1=kv, op0=ALU.mult, op1=ALU.add)
                    ins.then_inc(sem("state_ready"), 1)
            dve.wait_ge(sem("am_zero"), 1)
            for h in range(GLA_HEADS):
                dve.wait_ge(sem("att_ready"), h + 1)
                vector.copy_predicated(AM[:, h, :, :],
                                       tri.bitcast(mybir.dt.uint32).rearrange("p (o c) -> p o c", o=1).to_broadcast([P, NB, P]),
                                       PS[:, h, :].rearrange("p (n c) -> p n c", c=P)).then_inc(sem("am_ready"), 1)
            dve.wait_ge(sem("og_sum"), 1)
            vector.tensor_scalar(small[:, 0, :], PS[:, 0, 0:GLA_HEADS * NB], RMS_EPS, None, ALU.add
                                 ).then_inc(sem("og_variance"), 1)
            dve.wait_ge(sem("og_deviation"), 1)
            vector.reciprocal(small[:, 2, :], small[:, 1, :]).then_inc(sem("og_inverse"), 1)
            split(At(s.c + 5), words[s.c + 5])
            dve.wait_ge(sem("og_spread"), 1)
            for h in range(GLA_HEADS):
                vector.scalar_tensor_tensor(out=OG[:, h, :], in0=OG[:, h, :], scalar=vec("gla_out_norm"),
                                            in1=PS[:, 4 + h, :], op0=ALU.mult, op1=ALU.mult
                                            ).then_inc(sem("og_normed"), 1)
            dve.wait_ge(sem("og_normed"), GLA_HEADS)
            for k in range(4, 6):
                if k == 5:
                    split(At(s.c + 6), words[s.c + 6])
                dve.wait_ge(psum_free[k % 2], s.held[k % 2] + k // 2 + 1)
                if k == 5:
                    dve.wait_ge(sem("o2_lo"), 1)
                vector.tensor_tensor(TB[:, :, 0:SEQ], OG[:, 2 * k - 8:2 * k - 6, :], TA[:, :, 0:SEQ], ALU.mult
                                     ).then_inc(sem("og_gated"), 1)
                dve.wait_ge(sem("o2_hi"), k - 3)
                vector.tensor_tensor(O2_lo[:, 2 * k - 4:2 * k - 2, :], TB[:, :, 0:SEQ],
                                     O2_hi[:, 2 * k - 4:2 * k - 2, :].bitcast(FP32), ALU.subtract).then_inc(sem("o2_lo"), 1)
            dve.wait_ge(sem("o2_lo"), 2)
            merge("merge2", M_hi, M_lo)
            residual_sum("out2", 2, None, SEQ, META)
            norm(RMS_2)
            up_second("up3", SEQ)
            residual_sum("down3", 1, 0.5, SEQ, META)
            norm(RMS_OUT)


def kernel(**inputs):
    import ml_dtypes
    import numpy as np
    import concourse.bacc as bacc
    from concourse.bass_utils import run_bass_kernel_spmd

    a = {k: np.asarray(v) for k, v in inputs.items()}

    def chunked(w, width=2 * P):
        k, n = w.shape
        return w.reshape(k // P, P, n // width, width).transpose(2, 1, 0, 3).reshape(n // width, P, k // P * width)

    def down_chunks(w):
        return w.reshape(2, FH, P, KT, P).transpose(3, 0, 2, 1, 4).reshape(2 * KT, P, WD)

    def cols(v):
        return v.reshape(-1, P).T

    def features(x):
        return x.T.reshape(KT, P, -1).transpose(1, 0, 2)

    def merge_chunks(gate_one, gate_two, one, two):
        g1, g2, b = chunked(gate_one), chunked(gate_two), chunked(np.concatenate([one, two]))
        return [c[m] for m in range(4) for c in (g1, g2, b)]

    def up_chunks(first, second):
        f, s = chunked(first), chunked(second)
        return [c[m] for m in range(FH) for c in (f, s)]

    w1, w2 = a["w_in"][0], a["w_in_2"][0]
    fq, fk, fv, ff, bq, bk, bv, ga, gb = np.split(w1, np.cumsum([512, 512, 512, 8, 512, 512, 512, D]), axis=1)
    (aq, ak, av, gq, gk, gv, gr, low, ga2, gb2) = np.split(w2, np.cumsum([512, 128, 128, 256, 256, 512, 512, RANK, D]), axis=1)
    head_order = [h for t in range(4) for h in (t, 4 + t)]
    aq = aq.reshape(D, HEADS, HEAD)[:, head_order].reshape(D, 512)
    branch_att = a["w_branch_att_2"][0].reshape(HEADS, HEAD, D)[head_order].reshape(512, D)
    wts = []
    for v, q, k in ((fv, fq, fk), (bv, bq, bk)):
        wts += [*chunked(v), *chunked(q), *chunked(k)]
    wts += merge_chunks(ga, gb, a["w_br_fox"][0], a["w_br_chunk"][0])
    wts += [*chunked(a["w_out"][0])]
    wts += up_chunks(a["w_up"][0][:, :D_FF], a["w_up"][0][:, D_FF:])
    wts += up_chunks(a["ffn1_w_gate_2"][0], a["ffn1_w_up_2"][0])
    wts += [*chunked(aq), *chunked(np.concatenate([ak, av], axis=1))]
    wts += [*chunked(gq), *chunked(gk), *chunked(gv), *chunked(gr)]
    wts += merge_chunks(ga2, gb2, branch_att, a["w_branch_gla_2"][0])
    wts += [*chunked(a["w_out_2"][0])]
    wts += up_chunks(a["ffn2_w_gate_2"][0], a["ffn2_w_up_2"][0])
    f_at, low_at = 3 * 512, 512 + 256 + 512 + 1024
    forget = chunked(w1[:, f_at:f_at + P], P)[0].reshape(P, 2, WF).transpose(1, 0, 2)
    lowrank = chunked(w2[:, low_at:low_at + P], P)
    ident = np.eye(P, dtype=np.float32)
    key, query = np.arange(P)[:, None], np.arange(P)[None, :]
    within = (key <= query) & (key // CHUNK == query // CHUNK)
    cf = np.concatenate([ident, ident[::-1], within.astype(np.float32)], axis=1)
    causal = np.where(np.arange(P)[None, :] <= np.arange(P)[:, None], 0.0, NEG)
    cb = np.concatenate([ident, causal], axis=1).astype(ml_dtypes.bfloat16)
    qpos, kpos = np.arange(P)[:, None] + P, np.arange(2 * P)[None, :]
    reach = (kpos // CHUNK <= qpos // CHUNK) & (kpos // CHUNK >= qpos // CHUNK - 2)
    distance = np.where(reach, -np.abs(qpos - kpos).astype(np.float32), NEG)
    slopes = [2.0 ** -(h + 1) * ident for h in range(HEADS)]
    cw = np.concatenate([distance, *slopes], axis=1).astype(ml_dtypes.bfloat16)
    reset = np.ones((P, TOK), np.float32)
    reset[:, [0, *range(META, TOK, CHUNK)]] = 0.0
    f32 = np.float32
    parts = {
        "b_ada": cols(a["b_ada"][0]), "conv_w": cols(a["conv_w"][0]), "conv_b": cols(a["conv_b"][0]),
        "ln1_g": cols(a["ln1_g"][0]), "ln1_b": cols(a["ln1_b"][0]), "ln2_g": cols(a["ln2_g"][0]),
        "ln2_b": cols(a["ln2_b"][0]), "ffn1_norm": cols(a["ffn1_norm_2"][0]), "mix_norm": cols(a["mix_norm_2"][0]),
        "ffn2_norm": cols(a["ffn2_norm_2"][0]), "final_norm": cols(a["final_norm_2"]),
        "gla_gate_b": cols(a["gla_gate_b_2"][0]), "gla_out_norm": cols(a["gla_out_norm_2"][0]),
        "sinks": np.broadcast_to(a["att_sinks_2"][0], (P, HEADS)),
        "b_f": np.concatenate([a["b_f"][0], np.zeros(P - HEADS, f32)])[:, None],
    }
    rel = a["rel_bias"][0][:, 1:][:, ::-1]
    band_rel = np.concatenate([np.repeat(rel[:, :1], P - 1, axis=1), rel, rel[:, -1:]], axis=1)
    arrays = {
        "wts": np.stack(wts), "wfg": forget, "wlow": lowrank,
        "wdown": np.concatenate([down_chunks(a["w_down"][0]), down_chunks(a["ffn1_w_down_2"][0]),
                                 down_chunks(a["ffn2_w_down_2"][0])]),
        "wada": a["w_ada"][0].T.reshape(ADA, P, D), "cond": np.broadcast_to(a["c"][0], (P, D)),
        "vecs": np.concatenate([parts[n] for n, _ in VECS], axis=1),
        "xT": features(a["x"][0]), "metaT": features(a["meta_tokens_2"]), "gate_w": a["gla_gate_w_2"][0],
        "band_rel": band_rel, "cf": cf, "cb": cb, "cw": cw, "cs": reset,
    }
    arrays = {k: np.ascontiguousarray(v) for k, v in arrays.items()}
    nc = bacc.Bacc("TRN2", target_bir_lowering=False, num_devices=1)
    aps = {k: nc.dram_tensor(f"in_{k}", v.shape, mybir.dt.from_np(v.dtype), kind="ExternalInput").ap()
           for k, v in arrays.items()}
    out = nc.dram_tensor("out", (P, KT, SEQ), FP32, kind="ExternalOutput").ap()
    build_program(nc, **aps, out=out)
    r = run_bass_kernel_spmd(nc, [{f"in_{k}": v for k, v in arrays.items()}], core_ids=[0])
    y = r.results[0]["out"]
    return np.ascontiguousarray(y.transpose(2, 1, 0).reshape(1, SEQ, D))
```
